# Optimizing a Trainium2 kernel written in Bass

```python
import jax, jax.numpy as jnp
from jax import lax
import numpy as np

D_MODEL = 1024
BATCH = 1
SEQ = 512
DEPTH = 2
DEC_BATCH = 8
DEC_SEQ = 4
PAST_LEN = 1024
PAGE_SIZE = 128

N_AB_LAYERS = (DEPTH + 1) // 2
N_C_LAYERS = DEPTH // 2
N_HEADS_A = 8
HEAD_DIM_A = 64
ATTN_W = N_HEADS_A * HEAD_DIM_A
MOBA_BLOCK = 256
MOBA_TOPK = 3
Q_CHUNK = 32
CONV_CH = D_MODEL // 2
CONV_W = 3
IN_AB = 3 * ATTN_W + 3 * CONV_CH
CHUNK_C = 128
N_GROUPS_C = 8
C_WIDTH = D_MODEL
C_GROUP = C_WIDTH // N_GROUPS_C
D_FF = 4 * D_MODEL
EPS = 1e-6

kernel_name = "moba_shortconv_gmlp_hybrid_step"

def rms_norm(x, g):
    xf = x.astype(jnp.float32)
    xf = xf * lax.rsqrt(jnp.mean(xf * xf, axis=-1, keepdims=True) + EPS)
    return (xf * g.astype(jnp.float32)).astype(x.dtype)

def ada_terms(c, w, b):
    return jnp.split(jax.nn.silu(c) @ w + b, 6, axis=-1)

def modulate(h, shift, scale):
    return h * (1.0 + scale[:, None, :]) + shift[:, None, :]

def alibi_slopes():
    return jnp.exp2(-8.0 * jnp.arange(1, N_HEADS_A + 1, dtype=jnp.float32) / N_HEADS_A)

def moba_core(q, q_pos, sel, own_k, own_v, own_pos, own_ok, slopes):
    scale = HEAD_DIM_A ** -0.5
    sl = slopes[None, :, None, None]
    s_own = jnp.einsum('bhqd,bhmd->bhqm', q, own_k).astype(jnp.float32) * scale
    s_own = s_own - sl * (q_pos[:, None] - own_pos[None, :]).astype(jnp.float32)
    s_own = jnp.where(own_ok, s_own, -jnp.inf)
    if sel is None:
        p = jax.nn.softmax(s_own, axis=-1).astype(q.dtype)
        return jnp.einsum('bhqm,bhmd->bhqd', p, own_v)
    sel_k, sel_v, sel_pos, sel_ok = sel
    B, H, Q = s_own.shape[:3]
    s_sel = jnp.einsum('bhqd,bhqjld->bhqjl', q, sel_k).astype(jnp.float32) * scale
    s_sel = s_sel - sl[..., None] * (q_pos[:, None, None] - sel_pos).astype(jnp.float32)
    s_sel = jnp.where(sel_ok[..., None], s_sel, -jnp.inf)
    n_sel = s_sel.shape[3] * s_sel.shape[4]
    p = jax.nn.softmax(jnp.concatenate([s_sel.reshape(B, H, Q, n_sel), s_own], axis=-1), axis=-1)
    p_sel = p[..., :n_sel].reshape(s_sel.shape).astype(q.dtype)
    p_own = p[..., n_sel:].astype(q.dtype)
    return (jnp.einsum('bhqjl,bhqjld->bhqd', p_sel, sel_v)
            + jnp.einsum('bhqm,bhmd->bhqd', p_own, own_v))

def moba_prompt(q, k, v, slopes):
    B, S, H, Dh = q.shape
    nb = -(-S // MOBA_BLOCK)
    pad = nb * MOBA_BLOCK - S

    def to_blocks(t):
        t = jnp.pad(t, ((0, 0), (0, pad), (0, 0), (0, 0)))
        return t.reshape(B, nb, MOBA_BLOCK, H, Dh).transpose(0, 3, 1, 2, 4)

    kb, vb = to_blocks(k), to_blocks(v)
    k_mean = jnp.mean(kb.astype(jnp.float32), axis=3)
    qh = q.transpose(0, 2, 1, 3)
    n_sel = min(MOBA_TOPK, nb - 1)
    bi = jnp.arange(B)[:, None, None, None]
    hi = jnp.arange(H)[None, :, None, None]
    blk_ids = jnp.arange(nb)
    offs = jnp.arange(MOBA_BLOCK)

    def one_chunk(ci):
        start = ci * Q_CHUNK
        qc = lax.dynamic_slice_in_dim(qh, start, Q_CHUNK, axis=2)
        q_pos = start + jnp.arange(Q_CHUNK)
        ob = start // MOBA_BLOCK
        own_k = lax.dynamic_index_in_dim(kb, ob, axis=2, keepdims=False)
        own_v = lax.dynamic_index_in_dim(vb, ob, axis=2, keepdims=False)
        own_pos = ob * MOBA_BLOCK + offs
        own_ok = own_pos[None, :] <= q_pos[:, None]
        sel = None
        if n_sel > 0:
            cur = q_pos // MOBA_BLOCK
            gate = jnp.einsum('bhqd,bhnd->bhqn', qc.astype(jnp.float32), k_mean)
            gate = jnp.where(blk_ids[None, :] < cur[:, None], gate, -jnp.inf)
            _, idx = lax.top_k(gate, n_sel)
            sel = (kb[bi, hi, idx], vb[bi, hi, idx],
                   idx[..., None] * MOBA_BLOCK + offs,
                   jnp.arange(n_sel)[None, :] < cur[:, None])
        return moba_core(qc, q_pos, sel, own_k, own_v, own_pos, own_ok, slopes)

    out = lax.map(one_chunk, jnp.arange(S // Q_CHUNK))
    return out.transpose(1, 0, 3, 2, 4).reshape(B, S, H * Dh)

def moba_sample(q, k, v, cache_k, cache_v, page_table, slopes):
    Bd, T, H, Dh = q.shape
    n_pages = page_table.shape[1]
    past = n_pages * PAGE_SIZE
    nbp = past // MOBA_BLOCK
    own_start = nbp * MOBA_BLOCK
    own_page0 = own_start // PAGE_SIZE
    n_own_past = past - own_start
    qh = q.transpose(0, 2, 1, 3)
    q_pos = past + jnp.arange(T)
    own_pages = page_table[:, own_page0:]
    own_k = jnp.concatenate([cache_k[own_pages].reshape(Bd, n_own_past, H, Dh), k], axis=1).transpose(0, 2, 1, 3)
    own_v = jnp.concatenate([cache_v[own_pages].reshape(Bd, n_own_past, H, Dh), v], axis=1).transpose(0, 2, 1, 3)
    own_pos = own_start + jnp.arange(n_own_past + T)
    own_ok = own_pos[None, :] <= q_pos[:, None]
    sel = None
    n_sel = min(MOBA_TOPK, nbp)
    if n_sel > 0:
        ppb = MOBA_BLOCK // PAGE_SIZE
        k_rows = cache_k[page_table[:, :own_page0]].astype(jnp.float32)
        k_mean = jnp.mean(k_rows.reshape(Bd, nbp, MOBA_BLOCK, H, Dh), axis=2).transpose(0, 2, 1, 3)
        gate = jnp.einsum('bhqd,bhnd->bhqn', qh.astype(jnp.float32), k_mean)
        _, idx = lax.top_k(gate, n_sel)
        lp = idx[..., None] * ppb + jnp.arange(ppb)
        phys = page_table[jnp.arange(Bd)[:, None, None, None, None], lp]
        hi = jnp.arange(H)[None, :, None, None, None]
        shp = (Bd, H, T, n_sel, MOBA_BLOCK, Dh)
        sel = (cache_k[phys, :, hi, :].reshape(shp), cache_v[phys, :, hi, :].reshape(shp),
               idx[..., None] * MOBA_BLOCK + jnp.arange(MOBA_BLOCK),
               jnp.ones((T, n_sel), bool))
    out = moba_core(qh, q_pos, sel, own_k, own_v, own_pos, own_ok, slopes)
    return out.transpose(0, 2, 1, 3).reshape(Bd, T, H * Dh)

def short_conv(u, prev, w):
    T = u.shape[1]
    full = jnp.concatenate([prev, u], axis=1)
    y = full[:, 0:T] * w[0]
    for i in range(1, CONV_W):
        y = y + full[:, i:i + T] * w[i]
    return y, full[:, -(CONV_W - 1):]

def chunk_gmlp(h, w_in, g_v, w_s, b_s, w_out):
    B, T, _ = h.shape
    u, v = jnp.split(h @ w_in, 2, axis=-1)
    v = rms_norm(v, g_v)
    L = min(T, CHUNK_C)
    ws = jnp.where(jnp.tril(jnp.ones((CHUNK_C, CHUNK_C), bool)), w_s, 0.0).astype(h.dtype)[:, :L, :L]
    vr = v.reshape(B, T // L, L, N_GROUPS_C, C_GROUP)
    s = jnp.einsum('gts,bnsgd->bntgd', ws, vr) + jnp.swapaxes(b_s[:, :L], 0, 1)[:, :, None]
    return (u * s.reshape(B, T, C_WIDTH)) @ w_out, v

def trunk(x, c, paged, norm_g, w_ada, b_ada, w_in_ab, conv_w, w_out_ab, w_in_c, g_v, w_s, b_s,
          w_out_c, w_ff1, w_ff2, g_final):
    B, T, _ = x.shape
    slopes = alibi_slopes()
    splits = [ATTN_W, 2 * ATTN_W, 3 * ATTN_W, 3 * ATTN_W + CONV_CH, 3 * ATTN_W + 2 * CONV_CH]
    ks_, vs_, convs, cvs = [], [], [], []
    for layer in range(DEPTH):
        sh1, sc1, g1, sh2, sc2, g2 = ada_terms(c, w_ada[layer], b_ada[layer])
        h = modulate(rms_norm(x, norm_g[layer, 0]), sh1, sc1)
        if layer % 2 == 0:
            i = layer // 2
            q, k, v, bg, cg, xin = jnp.split(h @ w_in_ab[i], splits, axis=-1)
            q = q.reshape(B, T, N_HEADS_A, HEAD_DIM_A)
            k = k.reshape(B, T, N_HEADS_A, HEAD_DIM_A)
            v = v.reshape(B, T, N_HEADS_A, HEAD_DIM_A)
            if paged is None:
                attn = moba_prompt(q, k, v, slopes)
                prev = jnp.zeros((B, CONV_W - 1, CONV_CH), x.dtype)
                ks_.append(k.reshape(B * T // PAGE_SIZE, PAGE_SIZE, N_HEADS_A, HEAD_DIM_A))
                vs_.append(v.reshape(B * T // PAGE_SIZE, PAGE_SIZE, N_HEADS_A, HEAD_DIM_A))
            else:
                cache_k, cache_v, state_conv, page_table = paged
                attn = moba_sample(q, k, v, cache_k[i], cache_v[i], page_table, slopes)
                prev = state_conv[i]
                ks_.append(k)
                vs_.append(v)
            yc, conv_state = short_conv(cg * xin, prev, conv_w[i])
            convs.append(conv_state)
            mix = jnp.concatenate([attn, bg * yc], axis=-1) @ w_out_ab[i]
        else:
            j = layer // 2
            mix, v_rows = chunk_gmlp(h, w_in_c[j], g_v[j], w_s[j], b_s[j], w_out_c[j])
            cvs.append(v_rows)
        x = x + g1[:, None, :] * mix
        h = modulate(rms_norm(x, norm_g[layer, 1]), sh2, sc2)
        x = x + g2[:, None, :] * (jnp.square(jax.nn.relu(h @ w_ff1[layer])) @ w_ff2[layer])
    return rms_norm(x, g_final), ks_, vs_, convs, cvs

def setup_inputs(seed: int = 0) -> dict:
    key = jax.random.key(seed)
    ks = jax.random.split(key, 24)
    n_pages = PAST_LEN // PAGE_SIZE
    n_used = DEC_BATCH * n_pages
    n_pool = n_used + n_used // 4
    page_table = jax.random.permutation(ks[0], n_pool)[:n_used].reshape(DEC_BATCH, n_pages).astype(jnp.int32)

    def nrm(k, shape, scale=1.0):
        return jax.random.normal(k, shape, jnp.float32) * scale

    return {
        "x_prompt": nrm(ks[1], (BATCH, SEQ, D_MODEL)),
        "x_sample": nrm(ks[2], (DEC_BATCH, DEC_SEQ, D_MODEL)),
        "cache_k": nrm(ks[3], (N_AB_LAYERS, n_pool, PAGE_SIZE, N_HEADS_A, HEAD_DIM_A)),
        "cache_v": nrm(ks[4], (N_AB_LAYERS, n_pool, PAGE_SIZE, N_HEADS_A, HEAD_DIM_A)),
        "state_conv": nrm(ks[5], (N_AB_LAYERS, DEC_BATCH, CONV_W - 1, CONV_CH)),
        "page_table": page_table,
        "c_prompt": nrm(ks[6], (BATCH, D_MODEL)),
        "c_sample": nrm(ks[7], (DEC_BATCH, D_MODEL)),
        "norm_g": 1.0 + nrm(ks[8], (DEPTH, 2, D_MODEL), 0.02),
        "w_ada": nrm(ks[9], (DEPTH, D_MODEL, 6 * D_MODEL), D_MODEL ** -0.5),
        "b_ada": nrm(ks[10], (DEPTH, 6 * D_MODEL), 0.02),
        "w_in_ab": nrm(ks[11], (N_AB_LAYERS, D_MODEL, IN_AB), D_MODEL ** -0.5),
        "conv_w": nrm(ks[12], (N_AB_LAYERS, CONV_W, CONV_CH), CONV_W ** -0.5),
        "w_out_ab": nrm(ks[13], (N_AB_LAYERS, ATTN_W + CONV_CH, D_MODEL), (ATTN_W + CONV_CH) ** -0.5),
        "w_in_c": nrm(ks[14], (N_C_LAYERS, D_MODEL, 2 * C_WIDTH), D_MODEL ** -0.5),
        "g_v": 1.0 + nrm(ks[15], (N_C_LAYERS, C_WIDTH), 0.02),
        "w_s": nrm(ks[16], (N_C_LAYERS, N_GROUPS_C, CHUNK_C, CHUNK_C), CHUNK_C ** -0.5),
        "b_s": 1.0 + nrm(ks[17], (N_C_LAYERS, N_GROUPS_C, CHUNK_C), 0.02),
        "w_out_c": nrm(ks[18], (N_C_LAYERS, C_WIDTH, D_MODEL), C_WIDTH ** -0.5),
        "w_ff1": nrm(ks[19], (DEPTH, D_MODEL, D_FF), D_MODEL ** -0.5),
        "w_ff2": nrm(ks[20], (DEPTH, D_FF, D_MODEL), D_FF ** -0.5),
        "g_final": 1.0 + nrm(ks[21], (D_MODEL,), 0.02),
    }

def reference(x_prompt, x_sample, cache_k, cache_v, state_conv, page_table, c_prompt, c_sample,
              norm_g, w_ada, b_ada, w_in_ab, conv_w, w_out_ab, w_in_c, g_v, w_s, b_s, w_out_c,
              w_ff1, w_ff2, g_final):
    y_prompt, kp, vp, convp, _ = trunk(
        x_prompt, c_prompt, None, norm_g, w_ada, b_ada, w_in_ab, conv_w, w_out_ab,
        w_in_c, g_v, w_s, b_s, w_out_c, w_ff1, w_ff2, g_final)
    y_sample, ksm, vsm, convs, cvs = trunk(
        x_sample, c_sample, (cache_k, cache_v, state_conv, page_table), norm_g, w_ada, b_ada,
        w_in_ab, conv_w, w_out_ab, w_in_c, g_v, w_s, b_s, w_out_c, w_ff1, w_ff2, g_final)
    return (y_prompt, y_sample, jnp.stack(kp), jnp.stack(vp), jnp.stack(convp),
            jnp.stack(ksm), jnp.stack(vsm), jnp.stack(convs), jnp.stack(cvs))


_drawn_inputs = setup_inputs


def setup_inputs(seed=0):
    import zlib

    import numpy as np

    out = dict(_drawn_inputs(seed))
    spreads = {}
    factors = {'g_v': 2.883, 'b_s': 7.503, 'g_final': 2.733}
    for name, (base, spread) in spreads.items():
        noise = np.random.default_rng([zlib.crc32(name.encode()), seed]).standard_normal(out[name].shape)
        drawn = base * np.exp(spread * noise) if base else spread * noise
        out[name] = __import__('jax').numpy.asarray(drawn.astype(out[name].dtype))
    for name, factor in factors.items():
        out[name] = (out[name] * factor).astype(out[name].dtype)
    return out
```

```python
import concourse.bass as bass
from concourse import mybir
from contextlib import ExitStack

import numpy as np

D = 1024
KC = D // 128
NH, HD = 8, 64
SEQ = 512
NB, NT = 8, 4
PAGE, NPAGES = 128, 8
PAST = PAGE * NPAGES
POOL_PAGES = 80
HALF = 256 + 16
LA = 3
WSLOTS = 4
EPS = 1e-6
SCALE = HD ** -0.5
NEG = -1e30

T_AB, T_OUT, T_FF0, T_C, T_OUTC, T_FF1, T_END = 0, 24, 32, 96, 112, 120, 184


def trunk_kernel(nc, a, out):
    f32, f32r, i32 = mybir.dt.float32, mybir.dt.float32r, mybir.dt.int32
    ALU = mybir.AluOpType
    ACT = mybir.ActivationFunctionType
    AX = mybir.AxisListType
    ds = bass.ds

    top = [16512]

    def place(name, shape, dt=f32, at=None):
        size = 4 * int(np.prod(shape[1:]))
        if at is None:
            at = top[0]
            top[0] += (size + 31) // 32 * 32
        return nc.alloc_sbuf_tensor_at(name, shape, dt, offset=at)

    raw = place("raw_panels", [128, 2, KC, 256])
    w_hi = place("w_hi", [128, WSLOTS, KC, 128], f32r)
    w_lo = place("w_lo", [128, WSLOTS, KC, 128], f32r)
    x = place("x_resid", [128, KC, 2, HALF])
    H0 = top[0]
    h_hi = place("h_hi", [128, KC, 2, HALF], f32r)
    h_lo = place("h_lo", [128, KC, 2, HALF], f32r)
    kT = place("kT_pages", [128, 4, 4, 512], at=H0)
    A0 = top[0]
    ada_w = place("ada_w", [128, 2, 2048])
    v_own = place("v_own", [16, 2, 512], at=A0)
    k_own = place("k_own", [16, 2, 512], at=A0 + 4096)
    past_bias = place("past_bias", [128, PAST], at=A0 + 8192)
    k_tok = place("k_tok", [128, 4, 512], at=A0)
    C0 = A0 + 8192
    u_pad = place("u_pad", [128, 2 + SEQ], at=C0)
    u_smp = place("u_smp", [128, NB, 6], at=C0 + 2080)
    y_cv = place("y_cv", [128, 2, HALF], at=C0 + 2304)
    t_cv = place("t_cv", [128, 2, HALF], at=C0 + 4480)
    gv_row = place("gv_row", [128, D], at=A0)
    bs_row = place("bs_row", [128, 8, 128], at=A0 + 4096)
    ws_T = place("ws_T", [128, 8, 128], at=A0 + 8192)
    ws_blk = place("ws_blk", [32, 8, 32], at=A0 + 12288)
    B0 = top[0]
    ab = place("ab", [128, 24, 2, HALF])
    x_tok = place("x_tok", [128, 4, D], at=B0)
    xs_tok = place("xs_tok", [32, D], at=B0 + 16384)
    hid_hi = place("hid_hi", [128, KC, 2, HALF], f32r, at=B0)
    hid_lo = place("hid_lo", [128, KC, 2, HALF], f32r, at=B0 + 17408)
    y_T = place("y_T", [128, KC, 2, HALF], at=B0)
    ident = place("ident", [128, 128])
    ones = place("ones", [128, 128])
    dist = place("dist", [128, 512])
    head_mask = place("head_mask", [128, 512])
    own_bias = place("own_bias", [128, 16])
    slopes = place("slopes", [128, NH])
    rank4 = place("rank4", [128, 4])
    rep4 = place("rep4", [4, 32])
    blk_mask = place("blk_mask", [32, 32])
    tri = place("tri", [128, 128])
    vec_rows = place("vec_rows", [128, 128], at=A0)
    vec_rows2 = place("vec_rows2", [20, 128], at=A0 + 512)
    vec = place("vec", [128, 148])
    pages_ix = place("pages_ix", [1, 128], i32)
    c_rows = place("c_rows", [9, D], at=B0 + 20480)
    cT = place("cT", [128, KC, 32])
    c_exp = place("c_exp", [128, KC, 9])
    c_tr = place("c_tr", [128, KC, 9])
    adaT = place("adaT", [128, 96, 9])
    amod = place("amod", [128, KC, 9])
    eps_t = place("eps", [128, 1])
    s_att = place("s_att", [128, 4, 2, 16])
    cv_state = place("cv_state", [128, 4, 18])
    st_T = place("st_T", [128, 4, 16])
    rtmp = place("rtmp", [128, 2, 16])
    S0 = top[0]
    sq = place("sq", [128, 2, 2, HALF], at=S0)
    hf = place("hf", [128, 2, 2, HALF], at=S0 + 4352)
    lnt = place("lnt", [128, 2, HALF], at=S0 + 8704)
    rstd = place("rstd", [128, 2, HALF], at=S0 + 10880)
    uu = place("uu", [128, 2, 2, HALF], at=S0 + 13056)
    rel = place("rel", [128, 2, 2, HALF], at=S0)
    ffv = place("ffv", [128, 2, HALF], at=S0 + 4352)
    ada_sb = place("ada_sb", [128, 512], at=S0 + 17408)
    kv_ring = place("kv_ring", [128, 8, 512], at=S0)
    s_sb = place("s_sb", [128, PAST + 16], at=S0 + 16384)
    o_tmp = place("o_tmp", [128, 512], at=S0 + 16384)
    pT = place("pT", [128, 8, 128], at=S0 + 20544)
    q_bd = place("q_bd", [128, 4, 128], at=S0 + 24640)
    pT_own = place("pT_own", [16, 128], at=S0 + 26688)
    o2 = place("o2", [128, 2, HD], at=S0 + 27200)
    sm = place("sm", [128, 32], at=S0 + 27712)
    assert S0 + 27712 + 128 <= 229344, S0
    dist_h = place("dist_h", [128, 512], at=S0)
    P = place("P", [128, 2, 1280], at=S0 + 2048)
    PT = place("PT", [128, 1280], at=S0 + 12288)
    v_tok = place("v_tok", [128, 4, 512], at=S0 + 17408)
    pm = place("pm", [128, 2, 16], at=S0 + 25600)
    st_rows = place("st_rows", [16, 512], at=S0 + 25728)
    cv_out = place("cv_out", [18, 512], at=S0 + 25728)
    ws_raw = place("ws_raw", [128, 8, 128], at=S0)
    vn = place("vn", [128, 2, D], at=S0)
    vns = place("vns", [32, D], at=S0 + 8192)
    g1t = place("g1t", [128, 2, 512], at=S0 + 12288)
    g2t = place("g2t", [128, 2, 512], at=S0 + 16384)
    junk = place("junk", [128, D], at=S0 + 20480)
    vst = place("vst", [128, 3, 5], at=S0 + 24576)
    v_smp = place("v_smp", [128, KC, 32], at=S0 + 24704)
    y_smp = place("y_smp", [128, KC, 32], at=S0 + 21504)
    y_tok = place("y_tok", [128, 2, D], at=S0 + 13056)

    ctx = ExitStack()
    with ctx:
        G = [ctx.enter_context(nc.psum_tensor(f"gemm{i}", [128, 2, 512], f32)) for i in range(2)]
        AP = ctx.enter_context(nc.psum_tensor("ada_ps", [128, 512], f32))
        TP = ctx.enter_context(nc.psum_tensor("tp_ps", [128, 512], f32))
        ST = ctx.enter_context(nc.psum_tensor("stat_ps", [128, 2, 512], f32))

        def sem(name):
            return ctx.enter_context(nc.semaphore(name))

        raw_in = [sem("raw_in0"), sem("raw_in1")]
        hi_done, lo_done = sem("hi_done"), sem("lo_done")
        unit_done = sem("unit_done")
        psum_free = sem("psum_free")
        res_tmp, relu_r, relu_hi, hid_rdy = sem("res_tmp"), sem("relu_r"), sem("relu_hi"), sem("hid_rdy")
        ada_in = [sem("ada_in0"), sem("ada_in1")]
        ada_used, ada_copied, ada_tp, ada_T = sem("ada_used"), sem("ada_copied"), sem("ada_tp"), sem("ada_T")
        c_in, const_in, x_in = sem("c_in"), sem("const_in"), sem("x_in")
        pe_c, pe_vec, act_c, dve_c, dve_init, dve_vec = (sem("pe_c"), sem("pe_vec"), sem("act_c"), sem("dve_c"),
                                                        sem("dve_init"), sem("dve_vec"))
        pe_x, x_cp, x_cs = sem("pe_x"), sem("x_cp"), sem("x_cs")
        norm = [{k: sem(f"norm{n}_{k}") for k in ("mod", "sq", "st", "rs", "u", "s1", "s2", "hf", "hi", "h")}
                for n in range(4)]
        fin = {k: sem(f"fin_{k}") for k in ("sq", "st", "rs", "y", "tp", "cp")}
        out_done = sem("out_done")
        y_out = [sem("y_out0"), sem("y_out1")]
        tma_pe, tma_ev = sem("tma_pe"), sem("tma_ev")
        tmb_pe, tmb_ev = sem("tmb_pe"), sem("tmb_ev")
        bias_in, st_in, gm_in, ws_in = sem("bias_in"), sem("st_in"), sem("gm_in"), sem("ws_in")
        pg_in = [sem(f"pg_in{i}") for i in range(8)]
        page_free = sem("page_free")
        qz, q_rdy, kt_act, kt_dve, s_pe = sem("q_zero"), sem("q_rdy"), sem("kt_act"), sem("kt_dve"), sem("s_pe")
        sd, s_exp, p_pe, p_act, o2_pe = sem("s_dve"), sem("s_exp"), sem("p_pe"), sem("p_act"), sem("o2_pe")
        a_s, a_d, a_exp, a_tp, a_ev, a_o, a_hi, a_lo = (sem(n) for n in (
            "att_scores", "att_dve", "att_exp", "att_tp", "att_ev", "att_o", "att_hi", "att_lo"))
        a_ev2 = sem("att_ev_dve")
        cv, cv_hi, cv_lo, cv_pe, cv_ev = sem("conv_pool"), sem("conv_hi"), sem("conv_lo"), sem("conv_pe"), sem("conv_ev")
        v_rows = sem("v_rows")
        w_pe, w_dve, v_pe, v_act, v_dve, g_pe, g_d, g_hi, g_lo = (sem(n) for n in (
            "ws_pe", "ws_dve", "v_pe", "v_act", "v_dve", "g_pe", "g_dve", "g_hi", "g_lo"))

        panel = {"in_ab": a["w_in_ab"][0].rearrange("(k p) n -> p k n", p=128),
                 "out_ab": a["w_out_ab"][0].rearrange("(k p) n -> p k n", p=128),
                 "in_c": a["w_in_c"][0].rearrange("(k p) n -> p k n", p=128),
                 "out_c": a["w_out_c"][0].rearrange("(k p) n -> p k n", p=128)}
        ff1_v = [a["w_ff1"][l].rearrange("(k p) n -> p k n", p=128) for l in range(2)]
        ff2_v = [a["w_ff2"][l].rearrange("(k p) n -> p k n", p=128) for l in range(2)]
        gp = [G[s][:, :, 0:256] for s in range(2)]
        gs = [G[s][:, :, 256:272] for s in range(2)]
        BANKS = [G[0][:, 0, :], G[0][:, 1, :], G[1][:, 0, :], G[1][:, 1, :]]

        def bt(ap):
            return ap.rearrange("p h (b t) -> p h b t", t=NT)

        def per_row(rows):
            return rows.rearrange("p (h b) -> p h b", h=2).unsqueeze(3).broadcast_to([128, 2, 4, NT])

        def tok(buf, c, tt):
            return buf[:, c, tt // 2, 128 * (tt % 2):128 * (tt % 2) + 128]

        QOFF = [0, 128, 384, 768]

        SCB = [BANKS[0][:, 0:128], BANKS[0][:, 128:384], BANKS[1], BANKS[2]]
        PTO = [0, 512, 896, 1152]
        PTB = [ST[:, 0, :], ST[:, 1, :], AP[:, :], TP[:, :]]
        KTP = [G[1][:, 0, :], G[1][:, 1, :], AP[:, :], TP[:, :]]
        SD_EXP, SD_P, SD_O2, SD_STEPS = 13, 15, 18, 26
        AD_NEG, AD_STEPS = 6, 11
        CV_STEPS = 15
        N_STORES = 2 + 2 + 4 + 4 + 2 + 1
        N_CONST = 14
        KV_OUT = 4

        block = ctx.enter_context(nc.Block())

        @block.sync
        def _(sp):
            sp.dma_start(c_rows[0:1, :], a["c_prompt"]).then_inc(c_in, 16)
            sp.dma_start(c_rows[1:9, :], a["c_sample"]).then_inc(c_in, 16)
            for dst, src in ((ident, "k_ident"), (vec_rows, None), (vec_rows2, None), (dist, "k_dist"),
                             (head_mask, "k_head_mask"), (own_bias, "k_own_bias"), (slopes, "k_slopes"),
                             (rank4, "k_rank4"), (rep4, "k_rep4"), (blk_mask, "k_blk_mask"), (tri, "k_tri"),
                             (pages_ix, "page_order")):
                if dst is vec_rows:
                    sp.dma_start(vec_rows[0:96, :], a["b_ada"].rearrange("l (c n) -> (l c) n", n=128)).then_inc(const_in, 16)
                    sp.dma_start(vec_rows[96:128, :], a["norm_g"].rearrange("l s (c n) -> (l s c) n", n=128)).then_inc(const_in, 16)
                elif dst is vec_rows2:
                    sp.dma_start(vec_rows2[0:8, :], a["g_final"].rearrange("(c n) -> c n", n=128)).then_inc(const_in, 16)
                    sp.dma_start(vec_rows2[8:20, :], a["conv_w"].rearrange("l w (c n) -> (l w c) n", n=128)).then_inc(const_in, 16)
                else:
                    sp.dma_start(dst[:, :], a[src]).then_inc(const_in, 16)
            for tt in range(4):
                sp.dma_start(x_tok[:, tt, :], a["x_prompt"][0, 128 * tt:128 * tt + 128, :]).then_inc(x_in, 16)
            sp.dma_start(xs_tok[:, :], a["x_sample"].rearrange("b t n -> (b t) n")).then_inc(x_in, 16)

            def load_panel(p, slot, src, wait=True):
                if wait:
                    sp.wait_ge(lo_done, 2 * p - 2)
                sp.dma_start(raw[:, slot, :, :], src).then_inc(raw_in[slot], 16)

            def two_panels(p, view, col, rows=None):
                for s in range(2):
                    src = view[:, :, ds(col + 256 * s, 256)] if rows is None else view[:, ds(rows, KC), ds(col + 256 * s, 256)]
                    load_panel(p + s, s, src)

            load_panel(0, 0, panel["in_ab"][:, :, 0:256], wait=False)
            load_panel(1, 1, panel["in_ab"][:, :, 256:512], wait=False)
            with sp.Fori(1, 6) as i:
                two_panels(2 * i, panel["in_ab"], 512 * i)
            two_panels(12, panel["out_ab"], 0)

            sp.wait_ge(const_in, 16 * N_CONST)
            sp.wait_ge(norm[0]["h"], KC)
            with sp.Fori(0, 2) as g:
                for kv, cache in enumerate(("cache_k", "cache_v")):
                    pool_pages = a[cache][0].rearrange("a p h d -> a p (h d)")
                    with sp.Fori(0, 4) as q:
                        for s in range(8):
                            m = 64 * g + 32 * kv + 8 * q + s
                            sp.wait_ge(page_free, m + 1)
                            page = sp.value_load(pages_ix[0:1, ds(m, 1)], min_val=0, max_val=POOL_PAGES - 1)
                            sp.dma_start(kv_ring[:, s, :],
                                         pool_pages[ds(page, 1), :, :].rearrange("a p n -> (a p) n")).then_inc(pg_in[s], 16)
            two_panels(14, panel["out_ab"], 512)

            def load_ff(layer, p0):
                with sp.Fori(0, 4) as b:
                    with sp.Fori(0, 2) as i:
                        two_panels(p0 + 8 * b + 2 * i, ff1_v[layer], 1024 * b + 512 * i)
                    with sp.Fori(0, 2) as i:
                        two_panels(p0 + 8 * b + 4 + 2 * i, ff2_v[layer], 512 * i, rows=KC * b)

            load_ff(0, T_FF0 // 2)
            with sp.Fori(0, 4) as i:
                two_panels(T_C // 2 + 2 * i, panel["in_c"], 512 * i)
            with sp.Fori(0, 2) as i:
                two_panels(T_OUTC // 2 + 2 * i, panel["out_c"], 512 * i)
            load_ff(1, T_FF1 // 2)

            for tt in range(4):
                sp.wait_ge(fin["cp"], tt + 1)
                sp.dma_start(out["y_prompt"][0, 128 * tt:128 * tt + 128, :], y_tok[:, tt % 2, :]).then_inc(y_out[tt % 2], 16)
            sp.wait_ge(fin["cp"], 5)
            sp.dma_start(out["y_sample"].rearrange("b t n -> (b t) n"), y_tok[0:32, 0, :]).then_inc(y_out[0], 16)
            sp.wait_ge(y_out[0], 48)
            sp.wait_ge(y_out[1], 32)
            sp.wait_ge(out_done, 16 * N_STORES)

        @block.gpsimd
        def _(pool):
            def load_ada(c, slot, src, rows):
                pool.wait_ge(ada_used, c - 1)
                pool.dma_start(ada_w[:, slot, :], src).then_inc(ada_in[slot], 16)

            ada_v = [a["w_ada"][l].rearrange("(k p) (g n) -> g p k n", p=128, n=2048) for l in range(2)]
            pool.wait_ge(pe_vec, 1)
            for c in range(2):
                pool.dma_start(ada_w[:, c, :], ada_v[0][0, :, c, :]).then_inc(ada_in[c], 16)
            for c in range(2, KC):
                load_ada(c, c % 2, ada_v[0][0, :, c, :], None)
            for g in (1, 2):
                with pool.Fori(0, 4) as j:
                    for s in range(2):
                        load_ada(8 * g + 2 * j + s, s, ada_v[0][g, :, ds(2 * j + s, 1), :], None)

            pool.wait_ge(ada_used, 24)
            pool.dma_start(past_bias[:, :], a["k_past_bias"]).then_inc(bias_in, 16)
            for g in range(2):
                pool.wait_ge(tma_ev, g + 1)
                pool.dma_start(out["v_sample"][0, 4 * g:4 * g + 4].rearrange("b t h d -> (b t) (h d)"),
                               v_own[:, g, :]).then_inc(out_done, 16)
            for g in range(2):
                pool.wait_ge(tma_ev, g + 3)
                pool.dma_start(out["k_sample"][0, 4 * g:4 * g + 4].rearrange("b t h d -> (b t) (h d)"),
                               k_own[:, g, :]).then_inc(out_done, 16)

            pool.wait_ge(sd, 2 * SD_STEPS)
            pool.dma_start(st_rows[:, :], a["state_conv"][0].rearrange("b r n -> (b r) n")).then_inc(st_in, 16)
            pool.wait_ge(cv_ev, 1)
            n = [0]

            def did(ins):
                n[0] += 1
                ins.then_inc(cv, 1)

            def after():
                pool.wait_ge(cv, n[0])

            def smp(ap):
                return ap.rearrange("p (h b) t -> p h b t", h=2)

            for ch in range(4):
                cw = [vec[:, 128 + 8 + 4 * i + ch:128 + 9 + 4 * i + ch] for i in range(3)]
                if ch:
                    pool.wait_ge(cv_lo, ch)
                after()
                did(nc.gpsimd.memset(u_pad[:, 0:2], 0.0))
                did(nc.gpsimd.tensor_tensor(u_pad[:, 2:].rearrange("p (h n) -> p h n", h=2), ab[:, 16 + ch, :, 0:256],
                                            ab[:, 20 + ch, :, 0:256], ALU.mult))
                did(nc.gpsimd.tensor_copy(u_smp[:, :, 0:2], st_T[:, ch, :].rearrange("p (b r) -> p b r", r=2)))
                did(nc.gpsimd.tensor_tensor(smp(u_smp[:, :, 2:6]), bt(ab[:, 16 + ch, :, 256:272]),
                                            bt(ab[:, 20 + ch, :, 256:272]), ALU.mult))
                after()
                for i in range(3):
                    dst = y_cv if i == 0 else t_cv
                    did(nc.gpsimd.tensor_scalar(dst[:, :, 0:256], u_pad[:, i:i + SEQ].rearrange("p (h n) -> p h n", h=2),
                                                cw[i], None, ALU.mult))
                    did(nc.gpsimd.tensor_scalar(bt(dst[:, :, 256:272]), smp(u_smp[:, :, i:i + 4]), cw[i], None, ALU.mult))
                    after()
                    if i:
                        did(nc.gpsimd.tensor_tensor(y_cv[:, :, :], y_cv[:, :, :], t_cv[:, :, :], ALU.add))
                        after()
                did(nc.gpsimd.tensor_copy(cv_state[:, ch, 0:16].rearrange("p (b r) -> p b r", r=2), u_smp[:, :, 4:6]))
                did(nc.gpsimd.tensor_copy(cv_state[:, ch, 16:18], u_pad[:, SEQ:SEQ + 2]))
                did(nc.gpsimd.tensor_tensor(y_cv[:, :, :], y_cv[:, :, :], ab[:, 12 + ch, :, :], ALU.mult))
                assert n[0] == CV_STEPS * (ch + 1)

            for tt in range(4):
                pool.wait_ge(tmb_ev, tt + 1)
                pool.dma_start(out["v_prompt"][0, tt].rearrange("p h d -> p (h d)"), v_tok[:, tt, :]).then_inc(out_done, 16)
            for tt in range(4):
                pool.wait_ge(tmb_ev, tt + 5)
                pool.dma_start(out["k_prompt"][0, tt].rearrange("p h d -> p (h d)"), k_tok[:, tt, :]).then_inc(out_done, 16)
            pool.wait_ge(cv_ev, 2)
            pool.dma_start(out["conv_sample"][0].rearrange("b r n -> (b r) n"), cv_out[0:16, :]).then_inc(out_done, 16)
            pool.dma_start(out["conv_prompt"][0, 0], cv_out[16:18, :]).then_inc(out_done, 16)
            pool.wait_ge(out_done, 16 * 14)
            pool.wait_ge(cv_lo, 4)

            with pool.Fori(0, 3) as g:
                with pool.Fori(0, 4) as j:
                    for s in range(2):
                        load_ada(24 + 8 * g + 2 * j + s, s, ada_v[1][ds(g, 1), :, ds(2 * j + s, 1), :], None)

            pool.wait_ge(ada_used, 48)
            pool.dma_start(gv_row[:, :], a["g_v"].broadcast_to([128, D])).then_inc(gm_in, 16)
            pool.dma_start(bs_row[:, :, :].rearrange("p g t -> p (g t)"),
                           a["b_s"].rearrange("l g t -> l (g t)").broadcast_to([128, D])).then_inc(gm_in, 16)
            pool.wait_ge(norm[2]["h"], 8)
            pool.dma_start(ws_raw[:, :, :], a["w_s"][0].rearrange("g t s -> t g s")).then_inc(ws_in, 16)
            pool.wait_ge(v_dve, 5)
            pool.dma_start(out["cv_sample"][0].rearrange("b t n -> (b t) n"), vns[:, :]).then_inc(out_done, 16)

        @block.scalar
        def _(act):
            A = nc.scalar.activation

            def split_hi(u, slot):
                q, s = u
                act.wait_ge(raw_in[(s // 2) % 2], 16 * q + 16)
                if not (isinstance(q, int) and 4 * q + s < 4):
                    act.wait_ge(unit_done, 4 * q + s - 3)
                A(w_hi[:, s, :, :], raw[:, (s // 2) % 2, :, 128 * (s % 2):128 * (s % 2) + 128], ACT.Copy).then_inc(hi_done, 1)

            def ahead(q, s):
                return (q + (s + LA) // 4, (s + LA) % 4)

            def step_copy(q, s, idx, last=False):
                t = 4 * q + s
                split_hi(ahead(q, s), None)
                act.wait_ge(unit_done, t + 1)
                A(ab[:, ds(idx, 1), :, :], G[s % 2][:, :, 0:HALF].unsqueeze(1), ACT.Copy).then_inc(psum_free, 1)

            def step_relu(q, s, j, m):
                t = 4 * q + s
                split_hi(ahead(q, s), None)
                act.wait_ge(unit_done, t + 1)
                act.wait_ge(psum_free, t + 1)
                A(rel[:, s % 2, :, :], G[s % 2][:, :, 0:HALF], ACT.Relu).then_inc(relu_r, 1)
                act.wait_ge(relu_r, j + 1)
                A(hid_hi[:, ds(m, 1), :, :], rel[:, s % 2, :, :].unsqueeze(1), ACT.Square).then_inc(relu_hi, 1)

            def step_none(q, s, last):
                if not last:
                    split_hi(ahead(q, s), None)

            def ada_copy(g):
                act.wait_ge(ada_used, 8 * g + 8)
                act.wait_ge(ada_tp, g)
                A(ada_sb[:, :], AP[:, :], ACT.Copy).then_inc(ada_copied, 1)

            def norm_stats(s, ready):
                for c in range(KC):
                    ready(c)
                    if c >= 2:
                        act.wait_ge(s["st"], c - 1)
                    A(sq[:, c % 2, :, :], x[:, c, :, :], ACT.Square).then_inc(s["sq"], 1)
                act.wait_ge(s["st"], KC)
                A(lnt[:, :, :], ST[:, :, 0:HALF], ACT.Ln, bias=eps_t[:, 0:1], scale=1.0 / D).then_inc(s["rs"], 1)
                act.wait_ge(s["rs"], 1)
                A(rstd[:, :, :], lnt[:, :, :], ACT.Exp, scale=-0.5).then_inc(s["rs"], 1)

            def norm_apply(nn):
                s = norm[nn]
                sh = 48 * (nn // 2) + (0 if nn % 2 == 0 else 24)
                for c in range(KC):
                    act.wait_ge(s["u"], c + 1)
                    if c >= 2:
                        act.wait_ge(s["h"], c - 1)
                    A(hf[:, c % 2, :, 0:256], uu[:, c % 2, :, 0:256], ACT.Identity,
                      bias=adaT[:, sh + c, 0:1], scale=amod[:, c, 0:1]).then_inc(s["hf"], 1)
                    act.wait_ge(s["hf"], c + 1)
                    act.wait_ge(s["s2"], c + 1)
                    A(h_hi[:, c, :, :], hf[:, c % 2, :, :], ACT.Copy).then_inc(s["hi"], 1)

            act.wait_ge(pe_c, 1)
            act.wait_ge(dve_init, 3)
            A(c_exp[:, :, :], AP[:, 0:72].rearrange("p (k r) -> p k r", r=9), ACT.Exp, scale=-1.0).then_inc(act_c, 1)
            A(c_tr[:, :, :], AP[:, 0:72].rearrange("p (k r) -> p k r", r=9), ACT.Copy).then_inc(act_c, 1)
            for c in range(KC):
                act.wait_ge(pe_x, c + 1)
                A(x[:, c, :, 256:272], G[c % 2][:, 1, 0:32].rearrange("p (h n) -> p h n", h=2), ACT.Copy).then_inc(x_cs, 1)
            for u in range(LA):
                split_hi((0, u), None)

            def x_ready(c):
                act.wait_ge(x_cp, c + 1)
                act.wait_ge(x_cs, c + 1)
            norm_stats(norm[0], x_ready)
            ada_copy(0)
            norm_apply(0)

            with act.Fori(0, 2) as g:
                for s in range(8):
                    if s == 7:
                        ada_copy(g + 1)
                    step_copy(2 * g + s // 4, s % 4, 8 * g + s)
            with act.Fori(4, 6) as q:
                for s in range(4):
                    step_copy(q, s, 4 * q + s)

            for i in range(4):
                act.wait_ge(tma_pe, i + 1)
                dst = v_own if i < 2 else k_own
                A(dst[:, i % 2, :], BANKS[i][0:16, :], ACT.Copy).then_inc(tma_ev, 1)

            with act.Fori(0, 2) as g:
                for n in range(32):
                    if n % 2 == 0:
                        act.wait_ge(page_free, 64 * g + 8 + n + 1)
                        if n == 16:
                            act.wait_ge(s_pe, 2 * g + 1)
                        kh, b, pg = n // 16, n // 4 % 4, n % 4
                        A(kT[:, :, b, 128 * pg:128 * pg + 128], KTP[n % 4].rearrange("p (r n) -> p r n", r=4),
                          ACT.Copy).then_inc(kt_act, 1)
                act.wait_ge(sd, SD_STEPS * g + SD_EXP)
                A(s_sb[:, :], s_sb[:, :], ACT.Exp, bias=sm[:, 9:10], scale=SCALE, accum_out=sm[:, 10:11]).then_inc(s_exp, 1)
                for n in range(9):
                    act.wait_ge(p_pe, 9 * g + n + 1)
                    if n < 8:
                        A(pT[:, n, :], KTP[n % 4][:, 0:128], ACT.Copy).then_inc(p_act, 1)
                    else:
                        A(pT_own[:, :], KTP[0][0:16, 0:128], ACT.Copy).then_inc(p_act, 1)

            act.wait_ge(cv_pe, 1)
            A(st_T[:, :, :].rearrange("p c r -> p (c r)"), AP[:, 0:64], ACT.Copy).then_inc(cv_ev, 1)
            for i in range(8):
                act.wait_ge(tmb_pe, i + 1)
                dst = v_tok if i < 4 else k_tok
                if i == 4:
                    act.wait_ge(out_done, 16 * KV_OUT)
                A(dst[:, i % 4, :], BANKS[i % 4], ACT.Copy).then_inc(tmb_ev, 1)
            act.wait_ge(sd, 2 * SD_STEPS)
            A(h_hi[:, 0:4, :, 256:272].rearrange("p c h n -> p c h n"), s_att[:, :, :, :], ACT.Copy).then_inc(a_hi, 1)
            for h in range(NH + 1):
                if h < NH:
                    for i in range(4):
                        act.wait_ge(a_d, AD_STEPS * h + AD_NEG)
                        A(P[:, h % 2, QOFF[i]:QOFF[i] + 128 * (i + 1)], P[:, h % 2, QOFF[i]:QOFF[i] + 128 * (i + 1)], ACT.Exp,
                          bias=pm[:, h % 2, 4 + i:5 + i], scale=SCALE, accum_out=pm[:, h % 2, 8 + i:9 + i]).then_inc(a_exp, 1)
                if h >= 1:
                    g = h - 1
                    for j in (0, 2):
                        act.wait_ge(a_tp, 4 * g + j + 1)
                        if g:
                            act.wait_ge(a_o, g)
                        A(PT[:, PTO[j]:PTO[j] + 512 - 128 * j], PTB[j][:, 128 * j:512], ACT.Copy).then_inc(a_ev, 1)
                    if g % 2:
                        act.wait_ge(a_o, g + 1)
                        A(h_hi[:, g // 2, :, 0:256], BANKS[3].rearrange("p (h n) -> p h n", h=2), ACT.Copy).then_inc(a_hi, 1)
                if h and h % 2 == 0:
                    ch = h // 2 - 1
                    act.wait_ge(cv, CV_STEPS * (ch + 1))
                    A(h_hi[:, 4 + ch, :, :], y_cv[:, :, :], ACT.Copy).then_inc(cv_hi, 1)
            act.wait_ge(cv_pe, 2)
            A(cv_out[:, :], TP[0:18, :], ACT.Copy).then_inc(cv_ev, 1)

            with act.Fori(T_OUT // 4, T_FF0 // 4) as q:
                for s in range(4):
                    step_none(q, s, False)

            def resid_ready(T):
                return lambda c: act.wait_ge(psum_free, 2 + T - KC + c + 1)

            def ff(layer, T0, with_ada):
                J = 32 * layer
                q0 = T0 // 4

                def up(b, ada):
                    if ada:
                        for s in range(8):
                            if s == 7:
                                ada_copy(3 + b)
                            step_relu(q0 + 4 * b + s // 4, s % 4, J + 8 * b + s, s)
                    else:
                        with act.Fori(0, 2) as i:
                            for s in range(4):
                                step_relu(q0 + 4 * b + i, s, J + 8 * b + 4 * i + s, 4 * i + s)

                def down(b):
                    with act.Fori(0, 2) as i:
                        for s in range(4):
                            step_none(q0 + 4 * b + 2 + i, s, False)

                if with_ada:
                    with act.Fori(0, 3) as b:
                        up(b, True)
                        down(b)
                    up(3, False)
                    down(3)
                else:
                    with act.Fori(0, 3) as b:
                        up(b, False)
                        down(b)
                    up(3, False)
                    for i in range(2):
                        for s in range(4):
                            if T0 + 48 + 8 + 4 * i + s + LA < T_END:
                                step_none(q0 + 14 + i, s, False)

            norm_stats(norm[1], resid_ready(T_FF0))
            norm_apply(1)
            ff(0, T_FF0, True)
            norm_stats(norm[2], resid_ready(T_C))
            norm_apply(2)
            with act.Fori(T_C // 4, T_OUTC // 4) as q:
                for s in range(4):
                    step_copy(q, s, 4 * q + s - T_C)

            act.wait_ge(psum_free, 2 + T_OUTC)
            A(v_smp[:, :, :].rearrange("p c (h n) -> p c h n", h=2), ab[:, 8:16, :, 256:272], ACT.Copy).then_inc(v_rows, 1)
            for tt in range(5):
                m = 128 if tt < 4 else 32
                act.wait_ge(v_pe, tt + 1)
                A(junk[0:m, :], G[tt % 2][0:m, :, :].rearrange("p a n -> p (a n)"), ACT.Square,
                  accum_out=vst[0:m, 0, tt:tt + 1]).then_inc(v_act, 1)
                act.wait_ge(v_act, 3 * tt + 1)
                A(vst[0:m, 1, tt:tt + 1], vst[0:m, 0, tt:tt + 1], ACT.Ln, bias=eps_t[0:m, 0:1], scale=1.0 / D).then_inc(v_act, 1)
                act.wait_ge(v_act, 3 * tt + 2)
                A(vst[0:m, 2, tt:tt + 1], vst[0:m, 1, tt:tt + 1], ACT.Exp, scale=-0.5).then_inc(v_act, 1)
                if tt < 4:
                    for hb in range(2):
                        n = 2 * tt + hb
                        act.wait_ge(g_d, 2 * n + 2)
                        A(h_hi[:, 4 * hb:4 * hb + 4, tt // 2, 128 * (tt % 2):128 * (tt % 2) + 128],
                          g2t[:, n % 2, :].rearrange("p (g n) -> p g n", g=4), ACT.Copy).then_inc(g_hi, 1)
            act.wait_ge(g_d, 18)
            A(h_hi[:, :, :, 256:272], g2t[:, 0, 0:256].rearrange("p (g h n) -> p g h n", g=8, h=2), ACT.Copy).then_inc(g_hi, 1)

            with act.Fori(T_OUTC // 4, T_FF1 // 4) as q:
                for s in range(4):
                    step_none(q, s, False)
            act.wait_ge(out_done, 16 * N_STORES)
            norm_stats(norm[3], resid_ready(T_FF1))
            norm_apply(3)
            ff(1, T_FF1, False)

            norm_stats(fin, resid_ready(T_END))
            for tt in range(5):
                act.wait_ge(fin["tp"], tt + 1)
                if tt >= 2:
                    act.wait_ge(y_out[tt % 2], 16 * (tt // 2))
                m = 128 if tt < 4 else 32
                A(y_tok[0:m, tt % 2, :], G[tt % 2][0:m, :, :].rearrange("p a n -> p (a n)"), ACT.Copy).then_inc(fin["cp"], 1)

        @block.vector
        def _(dve):
            V = nc.vector

            def split_lo(u):
                q, s = u
                dve.wait_ge(hi_done, 4 * q + s + 1)
                V.tensor_tensor(w_lo[:, s, :, :], raw[:, (s // 2) % 2, :, 128 * (s % 2):128 * (s % 2) + 128],
                                w_hi[:, s, :, :].bitcast(f32), ALU.subtract).then_inc(lo_done, 1)

            def ahead(q, s):
                return (q + (s + LA) // 4, (s + LA) % 4)

            def step_copy(q, s):
                split_lo(ahead(q, s))

            def step_relu(q, s, j, m):
                t = 4 * q + s
                split_lo(ahead(q, s))
                dve.wait_ge(relu_r, j + 1)
                dve.wait_ge(hid_rdy, j)
                V.scalar_tensor_tensor(ffv[:, :, :], G[s % 2][:, :, 0:HALF], 0.0, rel[:, s % 2, :, :],
                                       ALU.max, ALU.mult).then_inc(psum_free, 1)
                dve.wait_ge(psum_free, t + 3)
                dve.wait_ge(relu_hi, j + 1)
                V.tensor_tensor(hid_lo[:, ds(m, 1), :, :], ffv[:, :, :].unsqueeze(1),
                                hid_hi[:, ds(m, 1), :, :].bitcast(f32), ALU.subtract).then_inc(hid_rdy, 1)

            def step_resid(q, s, r, m, gate, last=False):
                t = 4 * q + s
                if not last:
                    split_lo(ahead(q, s))
                dve.wait_ge(unit_done, t + 1)
                dve.wait_ge(psum_free, t + 2)
                V.tensor_tensor(bt(rtmp[:, :, :]), bt(gs[s % 2]),
                                per_row(adaT[:, ds(gate + m, 1), 1:9].rearrange("p a r -> p (a r)")), ALU.mult).then_inc(res_tmp, 1)
                xp = x[:, ds(m, 1), :, 0:256].rearrange("p a h n -> p (a h) n")
                V.scalar_tensor_tensor(xp, gp[s % 2], adaT[:, ds(gate + m, 1), 0:1].rearrange("p a r -> p (a r)"), xp,
                                       ALU.mult, ALU.add).then_inc(res_tmp, 1)
                dve.wait_ge(res_tmp, 2 * r + 1)
                xs = x[:, ds(m, 1), :, 256:272].rearrange("p a h n -> p (a h) n")
                V.tensor_tensor(xs, xs, rtmp[:, :, :], ALU.add).then_inc(psum_free, 1)

            def ada_turn(g):
                dve.wait_ge(ada_tp, g + 1)
                for m in range(4):
                    ins = V.tensor_tensor(
                        adaT[:, ds(16 * g, 16), :].rearrange("p (j m) r -> p j m r", m=4)[:, :, m, :],
                        TP[:, 128 * m:128 * m + 128].rearrange("p (j r) -> p j r", j=4)[:, :, 0:9],
                        vec[:, ds(16 * g, 16)].rearrange("p (j m) -> p j m", m=4)[:, :, m].unsqueeze(2).broadcast_to([128, 4, 9]),
                        ALU.add)
                ins.then_inc(ada_T, 1)

            def norm_apply(nn, groups):
                s = norm[nn]
                base = 48 * (nn // 2) + (0 if nn % 2 == 0 else 24)
                dve.wait_ge(ada_T, groups)
                V.scalar_tensor_tensor(amod[:, :, :], adaT[:, base + 8:base + 16, :], 1.0,
                                       vec[:, 96 + 8 * nn:104 + 8 * nn].unsqueeze(2).broadcast_to([128, KC, 9]),
                                       ALU.add, ALU.mult).then_inc(s["mod"], 1)
                dve.wait_ge(s["mod"], 1)
                dve.wait_ge(s["rs"], 2)

                def front(c):
                    if c >= 2:
                        dve.wait_ge(s["hf"], c - 1)
                        dve.wait_ge(s["h"], c - 1)
                    V.tensor_tensor(uu[:, c % 2, :, :], x[:, c, :, :], rstd[:, :, :], ALU.mult).then_inc(s["u"], 1)
                    dve.wait_ge(s["u"], c + 1)
                    V.tensor_tensor(bt(hf[:, c % 2, :, 256:272]), bt(uu[:, c % 2, :, 256:272]),
                                    per_row(amod[:, c, 1:9]), ALU.mult).then_inc(s["s1"], 1)
                    dve.wait_ge(s["s1"], c + 1)
                    V.tensor_tensor(bt(hf[:, c % 2, :, 256:272]), bt(hf[:, c % 2, :, 256:272]),
                                    per_row(adaT[:, base + c, 1:9]), ALU.add).then_inc(s["s2"], 1)

                front(0)
                for c in range(KC):
                    if c + 1 < KC:
                        front(c + 1)
                    dve.wait_ge(s["hi"], c + 1)
                    V.tensor_tensor(h_lo[:, c, :, :], hf[:, c % 2, :, :], h_hi[:, c, :, :].bitcast(f32),
                                    ALU.subtract).then_inc(s["h"], 1)

            V.memset(cT[:, :, :], 0.0).then_inc(dve_init, 1)
            V.memset(ones[:, :], 1.0).then_inc(dve_init, 1)
            V.memset(eps_t[:, :], EPS).then_inc(dve_init, 1)
            dve.wait_ge(act_c, 2)
            V.tensor_scalar(c_exp[:, :, :], c_exp[:, :, :], 1.0, None, ALU.add).then_inc(dve_c, 1)
            dve.wait_ge(dve_c, 1)
            V.reciprocal(c_exp[:, :, :], c_exp[:, :, :]).then_inc(dve_c, 1)
            dve.wait_ge(dve_c, 2)
            dve.wait_ge(dve_init, 3)
            V.tensor_tensor(cT[:, :, 0:9], c_tr[:, :, :], c_exp[:, :, :], ALU.mult).then_inc(dve_c, 1)
            dve.wait_ge(pe_vec, 1)
            V.tensor_copy(vec[:, :], TP[:, 0:148]).then_inc(dve_vec, 1)
            for c in range(KC):
                dve.wait_ge(pe_x, c + 1)
                V.tensor_copy(x[:, c, :, 0:256], G[c % 2][:, 0, :].rearrange("p (h n) -> p h n", h=2)).then_inc(x_cp, 1)
            for u in range(LA):
                split_lo((0, u))
            dve.wait_ge(dve_vec, 1)
            ada_turn(0)
            norm_apply(0, 1)

            with dve.Fori(0, 2) as g:
                for s in range(8):
                    step_copy(2 * g + s // 4, s % 4)
                ada_turn(g + 1)
            with dve.Fori(4, 6) as q:
                for s in range(4):
                    step_copy(q, s)

            dve.wait_ge(psum_free, 2 + 24)
            V.memset(q_bd[:, :, :], 0.0).then_inc(qz, 1)
            dve.wait_ge(qz, 1)
            with dve.Fori(0, 2) as g:
                base = SD_STEPS * g
                n = [0]

                def did(ins):
                    n[0] += 1
                    ins.then_inc(sd, 1)

                def after():
                    dve.wait_ge(sd, base + n[0])

                after()
                for hh in range(2):
                    rows = slice(64 * hh, 64 * hh + 64)
                    qd = q_bd[rows, :, :].rearrange("p r (b h t) -> p r b h t", b=4, h=8)
                    for pr in range(4):
                        ins = V.tensor_copy(qd[:, pr, :, 2 * pr + hh, :],
                                            ab[rows, pr, ds(g, 1), 256:272].rearrange("p a (b t) -> p (a b) t", t=NT))
                ins.then_inc(q_rdy, 1)
                for m in range(32):
                    if m % 2:
                        dve.wait_ge(page_free, 64 * g + 8 + m + 1)
                        if m == 17:
                            dve.wait_ge(s_pe, 2 * g + 1)
                        b, pg = m // 4 % 4, m % 4
                        V.tensor_copy(kT[:, :, b, 128 * pg:128 * pg + 128],
                                      KTP[m % 4].rearrange("p (r n) -> p r n", r=4)).then_inc(kt_dve, 1)
                dve.wait_ge(s_pe, 2 * g + 2)
                dve.wait_ge(bias_in, 16)
                did(V.tensor_reduce(sm[:, 0:4], ST[:, :, :].rearrange("p a (b n) -> p (a b) n", b=2), AX.X, ALU.add))
                did(V.tensor_tensor(s_sb[:, 0:PAST].rearrange("p (a n) -> p a n", a=2), ST[:, :, :],
                                    past_bias[:, :].rearrange("p (a n) -> p a n", a=2), ALU.add))
                did(V.tensor_tensor(s_sb[:, PAST:], G[0][:, 1, 0:16], own_bias[:, :], ALU.add))
                after()
                did(V.tensor_reduce(sm[:, 4:5], sm[:, 0:4], AX.X, ALU.min))
                after()
                did(V.scalar_tensor_tensor(sm[:, 12:16], sm[:, 0:4], sm[:, 4:5], rank4[:, :], ALU.is_le, ALU.mult))
                after()
                did(V.tensor_reduce(sm[:, 5:6], sm[:, 12:16], AX.X, ALU.max))
                after()
                did(V.tensor_scalar(sm[:, 16:20], sm[:, 12:16], sm[:, 5:6], NEG, ALU.is_equal, ALU.mult))
                after()
                for blk in range(4):
                    did(V.tensor_scalar(s_sb[:, 256 * blk:256 * blk + 256], s_sb[:, 256 * blk:256 * blk + 256],
                                        sm[:, 16 + blk:17 + blk], None, ALU.add))
                after()
                did(V.tensor_reduce(sm[:, 8:9], s_sb[:, :], AX.X, ALU.max))
                after()
                did(V.tensor_scalar(sm[:, 9:10], sm[:, 8:9], -SCALE, None, ALU.mult))
                assert n[0] == SD_EXP, n
                dve.wait_ge(s_exp, g + 1)
                did(V.reciprocal(sm[:, 11:12], sm[:, 10:11]))
                after()
                did(V.tensor_scalar(s_sb[:, :], s_sb[:, :], sm[:, 11:12], None, ALU.mult))
                assert n[0] == SD_P, n
                dve.wait_ge(page_free, 64 * g + 8 + 64)
                did(V.tensor_tensor(o_tmp[:, :], G[0][:, 0, :], head_mask[:, :], ALU.mult))
                after()
                for dup in range(2):
                    did(V.tensor_reduce(o2[:, dup, :], o_tmp[:, :].rearrange("p (h d) -> p d h", h=8), AX.X, ALU.add))
                assert n[0] == SD_O2, n
                dve.wait_ge(o2_pe, g + 1)
                for hh in range(2):
                    rows = slice(64 * hh, 64 * hh + 64)
                    src = TP[rows, 0:128].rearrange("p (b h t) -> p b h t", b=4, h=8)
                    for pr in range(4):
                        did(V.tensor_copy(s_att[rows, pr, ds(g, 1), :].rearrange("p a (b t) -> p (a b) t", t=NT),
                                          src[:, :, 2 * pr + hh, :]))
                assert n[0] == SD_STEPS, n

            dve.wait_ge(tmb_ev, 8)
            dve.wait_ge(a_hi, 1)
            V.tensor_tensor(h_lo[:, 0:4, :, 256:272].rearrange("p c h n -> p c h n"), s_att[:, :, :, :],
                            h_hi[:, 0:4, :, 256:272].bitcast(f32), ALU.subtract).then_inc(a_lo, 1)
            nd = [0]

            def did(ins):
                nd[0] += 1
                ins.then_inc(a_d, 1)

            for h in range(NH + 1):
                if h < NH:
                    hp = h % 2
                    nd[0] = AD_STEPS * h
                    dve.wait_ge(a_d, nd[0]) if h else None
                    did(V.tensor_scalar(dist_h[:, :], dist[:, :], slopes[:, h:h + 1], None, ALU.mult))
                    dve.wait_ge(a_d, nd[0])
                    if h >= 2:
                        dve.wait_ge(a_tp, 4 * (h - 1))
                    for i in range(4):
                        w = 128 * (i + 1)
                        dve.wait_ge(a_s, 4 * h + max(i, 1) + 1)
                        did(V.tensor_tensor_reduce(
                            out=P[:, hp, QOFF[i]:QOFF[i] + w], in0=SCB[i][:, 0:w], in1=dist_h[:, 384 - 128 * i:512],
                            scale=1.0, scalar=-3e38, op0=ALU.add, op1=ALU.max, accum_out=pm[:, hp, i:i + 1]))
                    dve.wait_ge(a_d, nd[0])
                    did(V.tensor_scalar(pm[:, hp, 4:8], pm[:, hp, 0:4], -SCALE, None, ALU.mult))
                    assert nd[0] - AD_STEPS * h == AD_NEG
                    dve.wait_ge(a_exp, 4 * h + 4)
                    did(V.reciprocal(pm[:, hp, 12:16], pm[:, hp, 8:12]))
                    dve.wait_ge(a_d, nd[0])
                    for i in range(4):
                        sl = P[:, hp, QOFF[i]:QOFF[i] + 128 * (i + 1)]
                        did(V.tensor_scalar(sl, sl, pm[:, hp, 12 + i:13 + i], None, ALU.mult))
                    assert nd[0] == AD_STEPS * (h + 1)
                if h >= 1:
                    g = h - 1
                    for j in (1, 3):
                        dve.wait_ge(a_tp, 4 * g + j + 1)
                        if g:
                            dve.wait_ge(a_o, g)
                        V.tensor_copy(PT[:, PTO[j]:PTO[j] + 512 - 128 * j], PTB[j][:, 128 * j:512]).then_inc(a_ev2, 1)
                    if g % 2:
                        dve.wait_ge(a_hi, 2 + g // 2)
                        V.tensor_tensor(h_lo[:, g // 2, :, 0:256], BANKS[3].rearrange("p (h n) -> p h n", h=2),
                                        h_hi[:, g // 2, :, 0:256].bitcast(f32), ALU.subtract).then_inc(a_lo, 1)
                if h and h % 2 == 0:
                    ch = h // 2 - 1
                    dve.wait_ge(cv_hi, ch + 1)
                    V.tensor_tensor(h_lo[:, 4 + ch, :, :], y_cv[:, :, :], h_hi[:, 4 + ch, :, :].bitcast(f32),
                                    ALU.subtract).then_inc(cv_lo, 1)

            with dve.Fori(0, 2) as i:
                for s in range(4):
                    step_resid(T_OUT // 4 + i, s, 4 * i + s, 4 * i + s, 16)

            def ff(layer, T0, R0, with_ada):
                J = 32 * layer
                q0 = T0 // 4
                gate = 48 * layer + 40

                def up(b, ada):
                    if ada:
                        for s in range(8):
                            step_relu(q0 + 4 * b + s // 4, s % 4, J + 8 * b + s, s)
                        ada_turn(3 + b)
                    else:
                        with dve.Fori(0, 2) as i:
                            for s in range(4):
                                step_relu(q0 + 4 * b + i, s, J + 8 * b + 4 * i + s, 4 * i + s)

                def down(b):
                    with dve.Fori(0, 2) as i:
                        for s in range(4):
                            step_resid(q0 + 4 * b + 2 + i, s, R0 + 8 * b + 4 * i + s, 4 * i + s, gate)

                if with_ada:
                    with dve.Fori(0, 3) as b:
                        up(b, True)
                        down(b)
                    up(3, False)
                    down(3)
                else:
                    with dve.Fori(0, 3) as b:
                        up(b, False)
                        down(b)
                    up(3, False)
                    for i in range(2):
                        for s in range(4):
                            step_resid(q0 + 14 + i, s, R0 + 24 + 4 * i + s, 4 * i + s, gate,
                                       last=not T0 + 48 + 8 + 4 * i + s + LA < T_END)

            norm_apply(1, 3)
            ff(0, T_FF0, 8, True)
            norm_apply(2, 4)

            with dve.Fori(T_C // 4, T_OUTC // 4) as q:
                for s in range(4):
                    step_copy(q, s)

            dve.wait_ge(w_pe, 1)
            V.tensor_tensor(ws_T[:, 0:4, :], ST[:, 0, :].rearrange("p (g t) -> p g t", g=4),
                            tri[:, :].unsqueeze(1).broadcast_to([128, 4, 128]), ALU.mult).then_inc(w_dve, 1)
            V.tensor_tensor(ws_T[:, 4:8, :], ST[:, 1, :].rearrange("p (g t) -> p g t", g=4),
                            tri[:, :].unsqueeze(1).broadcast_to([128, 4, 128]), ALU.mult).then_inc(w_dve, 1)
            dve.wait_ge(w_pe, 2)
            V.tensor_tensor(ws_blk[:, :, :].rearrange("p g (b t) -> p g b t", t=NT),
                            AP[0:32, 0:32].rearrange("p (g t) -> p g t", t=NT).unsqueeze(2).broadcast_to([32, 8, 8, NT]),
                            blk_mask[:, :].rearrange("p (b t) -> p b t", t=NT).unsqueeze(1).broadcast_to([32, 8, 8, NT]),
                            ALU.mult).then_inc(w_dve, 1)
            dve.wait_ge(gm_in, 32)
            for tt in range(5):
                m = 128 if tt < 4 else 32
                dve.wait_ge(v_act, 3 * tt + 3)
                if tt >= 2:
                    dve.wait_ge(g_pe, 2 * (tt - 1))
                dst = vn[:, tt % 2, :] if tt < 4 else vns[:, :]
                V.scalar_tensor_tensor(dst, G[tt % 2][0:m, :, :].rearrange("p a n -> p (a n)"), vst[0:m, 2, tt:tt + 1],
                                       gv_row[0:m, :], ALU.mult, ALU.mult).then_inc(v_dve, 1)
                if tt == 4:
                    break
                for hb in range(2):
                    n = 2 * tt + hb
                    dve.wait_ge(g_pe, n + 1)
                    g4 = slice(4 * hb, 4 * hb + 4)
                    V.tensor_tensor(g1t[:, n % 2, :].rearrange("p (g n) -> p g n", g=4),
                                    ST[:, n % 2, :].rearrange("p (g n) -> p g n", g=4), bs_row[:, g4, :], ALU.add).then_inc(g_d, 1)
                    dve.wait_ge(g_d, 2 * n + 1)
                    if n >= 2:
                        dve.wait_ge(g_lo, n - 1)
                    V.tensor_tensor(g2t[:, n % 2, :].rearrange("p (g n) -> p g n", g=4),
                                    g1t[:, n % 2, :].rearrange("p (g n) -> p g n", g=4),
                                    ab[:, g4, tt // 2, 128 * (tt % 2):128 * (tt % 2) + 128], ALU.mult).then_inc(g_d, 1)
                    dve.wait_ge(g_hi, n + 1)
                    V.tensor_tensor(h_lo[:, g4, tt // 2, 128 * (tt % 2):128 * (tt % 2) + 128],
                                    g2t[:, n % 2, :].rearrange("p (g n) -> p g n", g=4),
                                    h_hi[:, g4, tt // 2, 128 * (tt % 2):128 * (tt % 2) + 128].bitcast(f32),
                                    ALU.subtract).then_inc(g_lo, 1)
            dve.wait_ge(g_pe, 9)
            V.tensor_tensor(g1t[:, 0, 0:256].rearrange("p (g b t) -> p g b t", g=8, t=NT),
                            AP[:, 0:256].rearrange("p (g b t) -> p g b t", g=8, t=NT),
                            bs_row[:, :, 0:NT].unsqueeze(2).broadcast_to([128, 8, 8, NT]), ALU.add).then_inc(g_d, 1)
            dve.wait_ge(g_d, 17)
            dve.wait_ge(g_lo, 8)
            V.tensor_tensor(g2t[:, 0, 0:256].rearrange("p (g h n) -> p g h n", g=8, h=2),
                            g1t[:, 0, 0:256].rearrange("p (g h n) -> p g h n", g=8, h=2),
                            ab[:, 0:8, :, 256:272], ALU.mult).then_inc(g_d, 1)
            dve.wait_ge(g_hi, 9)
            V.tensor_tensor(h_lo[:, :, :, 256:272], g2t[:, 0, 0:256].rearrange("p (g h n) -> p g h n", g=8, h=2),
                            h_hi[:, :, :, 256:272].bitcast(f32), ALU.subtract).then_inc(g_lo, 1)

            with dve.Fori(0, 2) as i:
                for s in range(4):
                    step_resid(T_OUTC // 4 + i, s, 40 + 4 * i + s, 4 * i + s, 48 + 16)
            norm_apply(3, 6)
            ff(1, T_FF1, 48, False)

            dve.wait_ge(fin["rs"], 2)
            for c in range(KC):
                V.scalar_tensor_tensor(y_smp[:, c, :].rearrange("p (h n) -> p h n", h=2), x[:, c, :, 256:272],
                                       vec[:, 128 + c:129 + c], rstd[:, :, 256:272], ALU.mult, ALU.mult)
                V.scalar_tensor_tensor(y_T[:, c, :, 0:256], x[:, c, :, 0:256], vec[:, 128 + c:129 + c],
                                       rstd[:, :, 0:256], ALU.mult, ALU.mult).then_inc(fin["y"], 1)

        @block.tensor
        def _(pe):
            mm, tr = nc.tensor.matmul, nc.tensor.transpose

            def unit(q, s, rhs_hi, rhs_lo, wait_k=None):
                t = 4 * q + s
                pe.wait_ge(lo_done, t + 1)
                pe.wait_ge(psum_free, t + 1)
                for k in range(KC):
                    if wait_k:
                        wait_k(k)
                    for w, r in ((w_hi, rhs_hi), (w_hi, rhs_lo), (w_lo, rhs_hi)):
                        for half in range(2):
                            ins = mm(G[s % 2][:, half, 0:HALF], w[:, s, k, :], r[:, k, half, :],
                                     start=(k == 0 and w is w_hi and r is rhs_hi), stop=(k == KC - 1 and w is w_lo))
                ins.then_inc(unit_done, 1)

            def ada_chunk(g, k, first=False):
                pe.wait_ge(ada_in[k % 2], 64 * g + 16 * (k // 2) + 16)
                if k == 0:
                    pe.wait_ge(ada_copied, g)
                for j in range(4):
                    ins = mm(AP[32 * j:32 * j + 32, :], cT[:, k, :], ada_w[:, k % 2, 512 * j:512 * j + 512],
                             start=(k == 0), stop=(k == KC - 1))
                ins.then_inc(ada_used, 1)

            def ada_turn(g):
                pe.wait_ge(ada_copied, g + 1)
                pe.wait_ge(ada_T, g)
                for m in range(4):
                    ins = tr(TP[:, 128 * m:128 * m + 128], ada_sb[:, 128 * m:128 * m + 128], ident[:, :])
                ins.then_inc(ada_tp, 1)

            def norm_stats(s):
                for c in range(KC):
                    pe.wait_ge(s["sq"], c + 1)
                    for half in range(2):
                        ins = mm(ST[:, half, 0:HALF], ones[:, :], sq[:, c % 2, half, :], start=(c == 0), stop=(c == KC - 1))
                    ins.then_inc(s["st"], 1)

            pe.sem_inc(psum_free, 2)
            pe.sem_inc(page_free, 8)
            pe.wait_ge(c_in, 32)
            pe.wait_ge(const_in, 16 * N_CONST)
            for k in range(KC):
                ins = tr(AP[:, 9 * k:9 * k + 9], c_rows[:, 128 * k:128 * k + 128], ident[0:9, 0:9])
            ins.then_inc(pe_c, 1)
            tr(TP[:, 0:128], vec_rows[:, :], ident[:, :])
            tr(TP[:, 128:148], vec_rows2[:, :], ident[0:20, 0:20]).then_inc(pe_vec, 1)
            pe.wait_ge(x_in, 80)
            for c in range(KC):
                if c >= 2:
                    pe.wait_ge(x_cp, c - 1)
                    pe.wait_ge(x_cs, c - 1)
                for tt in range(4):
                    tr(G[c % 2][:, 0, 128 * tt:128 * tt + 128], x_tok[:, tt, 128 * c:128 * c + 128], ident[:, :])
                tr(G[c % 2][:, 1, 0:32], xs_tok[:, 128 * c:128 * c + 128], ident[0:32, 0:32]).then_inc(pe_x, 1)
            pe.wait_ge(dve_init, 3)
            norm_stats(norm[0])
            pe.wait_ge(dve_c, 3)
            for k in range(KC):
                ada_chunk(0, k)
            pe.wait_ge(dve_vec, 1)
            ada_turn(0)

            def from_norm(n):
                return lambda k: pe.wait_ge(norm[n]["h"], k + 1)

            with pe.Fori(0, 2) as g:
                for s in range(8):
                    ada_chunk(g + 1, s)
                    unit(2 * g + s // 4, s % 4, h_hi, h_lo, from_norm(0))
                ada_turn(g + 1)
            with pe.Fori(4, 6) as q:
                for s in range(4):
                    unit(q, s, h_hi, h_lo)

            pe.wait_ge(psum_free, 2 + 24)
            for i in range(4):
                c0, g = (8, i) if i < 2 else (4, i - 2)
                for ch in range(4):
                    ins = tr(BANKS[i][0:16, 128 * ch:128 * ch + 128], ab[:, c0 + ch, g, 256:272], ident[:, :])
                ins.then_inc(tma_pe, 1)

            pe.wait_ge(tma_ev, 4)
            pe.wait_ge(ada_T, 3)
            with pe.Fori(0, 2) as g:
                pe.wait_ge(q_rdy, g + 1)
                pe.wait_ge(sd, SD_STEPS * g)
                for pr in range(4):
                    mm(G[0][:, 1, 0:16], q_bd[:, pr, :], ab[:, 4 + pr, ds(g, 1), 256:272].rearrange("p a n -> p (a n)"),
                       start=(pr == 0), stop=(pr == 3))
                for n in range(32):
                    slot = n % 8
                    kh = n // 16
                    pe.wait_ge(pg_in[slot], 128 * g + 16 * (n // 8) + 16)
                    if n >= 4:
                        pe.wait_ge(kt_dve if n % 2 else kt_act, 16 * g + (n - 4) // 2 + 1)
                    for pr in range(4):
                        ins = tr(KTP[n % 4][:, 128 * pr:128 * pr + 128], kv_ring[:, slot, 128 * pr:128 * pr + 128], ident[:, :])
                    ins.then_inc(page_free, 1)
                    if n % 16 == 15:
                        pe.wait_ge(kt_act, 16 * g + 8 * kh + 8)
                        pe.wait_ge(kt_dve, 16 * g + 8 * kh + 8)
                        for pr in range(4):
                            for b in range(4):
                                ins = mm(ST[32 * b:32 * b + 32, kh, :], q_bd[:, pr, 32 * b:32 * b + 32], kT[:, pr, b, :],
                                         start=(pr == 0), stop=(pr == 3))
                        ins.then_inc(s_pe, 1)
                pe.wait_ge(sd, SD_STEPS * g + SD_P)
                for n in range(9):
                    if n >= 4:
                        pe.wait_ge(p_act, 9 * g + n - 3)
                    if n < 8:
                        tr(KTP[n % 4][:, 0:128], s_sb[:, 128 * n:128 * n + 128], ident[:, :]).then_inc(p_pe, 1)
                    else:
                        tr(KTP[0][0:16, 0:128], s_sb[:, PAST:], ident[:, :]).then_inc(p_pe, 1)
                pe.wait_ge(p_act, 9 * g + 9)
                mm(G[0][:, 0, :], pT_own[:, :], v_own[:, ds(g, 1), :].rearrange("p a n -> p (a n)"), start=True, stop=False,
                   skip_group_check=True)
                for n in range(32):
                    slot, j, b = n % 8, n // 4, n % 4
                    pe.wait_ge(pg_in[slot], 128 * g + 64 + 16 * (n // 8) + 16)
                    mm(G[0][32 * b:32 * b + 32, 0, :], pT[:, j, 32 * b:32 * b + 32], kv_ring[:, slot, :],
                       start=False, stop=(j == 7), skip_group_check=True).then_inc(page_free, 1)
                pe.wait_ge(sd, SD_STEPS * g + SD_O2)
                tr(TP[:, 0:128], o2[:, :, :].rearrange("p a d -> p (a d)"), ident[:, :]).then_inc(o2_pe, 1)

            pe.wait_ge(st_in, 16)
            for ch in range(4):
                ins = tr(AP[:, 16 * ch:16 * ch + 16], st_rows[:, 128 * ch:128 * ch + 128], ident[0:16, 0:16])
            ins.then_inc(cv_pe, 1)
            pe.wait_ge(sd, 2 * SD_STEPS)
            for i in range(8):
                if i >= 4:
                    pe.wait_ge(tmb_ev, i - 3)
                for ch in range(4):
                    ins = tr(BANKS[i % 4][:, 128 * ch:128 * ch + 128], tok(ab, (8 if i < 4 else 4) + ch, i % 4), ident[:, :])
                ins.then_inc(tmb_pe, 1)
            pe.wait_ge(tmb_ev, 8)
            pe.wait_ge(cv_ev, 1)

            def scores(h):
                rows, pr = slice(64 * (h % 2), 64 * (h % 2) + 64), h // 2
                if h:
                    pe.wait_ge(a_d, AD_STEPS * (h - 1) + 5)
                for i in range(4):
                    q = tok(ab, pr, i)[rows, :]
                    if i == 0:
                        ins = mm(SCB[i], q, ab[rows, 4 + pr, 0, 0:128], start=True, stop=True)
                    elif i == 1:
                        ins = mm(SCB[i], q, ab[rows, 4 + pr, 0, 0:256], start=True, stop=True)
                    elif i == 2:
                        mm(SCB[i][:, 0:256], q, ab[rows, 4 + pr, 0, 0:256], start=True, stop=True)
                        ins = mm(SCB[i][:, 256:384], q, ab[rows, 4 + pr, 1, 0:128], start=True, stop=True)
                    else:
                        ins = mm(SCB[i], q, ab[rows, 4 + pr, :, 0:256], start=True, stop=True)
                    ins.then_inc(a_s, 1)

            scores(0)
            for h in range(NH):
                if h + 1 < NH:
                    scores(h + 1)
                pe.wait_ge(a_d, AD_STEPS * (h + 1))
                for j in range(4):
                    if h:
                        pe.wait_ge(a_ev2 if j % 2 else a_ev, 2 * (h - 1) + j // 2 + 1)
                    for i in range(j, 4):
                        ins = tr(PTB[j][:, 128 * i:128 * i + 128], P[:, h % 2, QOFF[i] + 128 * j:QOFF[i] + 128 * j + 128],
                                 ident[:, :])
                    ins.then_inc(a_tp, 1)
                pe.wait_ge(a_ev, 2 * h + 2)
                pe.wait_ge(a_ev2, 2 * h + 2)
                if h % 2 == 0 and h:
                    pe.wait_ge(a_lo, 1 + h // 2)
                rows = slice(64 * (h % 2), 64 * (h % 2) + 64)
                for j in range(4):
                    ins = mm(BANKS[3][rows, 128 * j:512], v_tok[:, j, 64 * h:64 * h + 64], PT[:, PTO[j]:PTO[j] + 512 - 128 * j],
                             start=(j == 0), stop=(j == 3), skip_group_check=True)
                ins.then_inc(a_o, 1)
            pe.wait_ge(cv, 4 * CV_STEPS)
            for ch in range(4):
                ins = tr(TP[0:18, 128 * ch:128 * ch + 128], cv_state[:, ch, :], ident[:, :])
            ins.then_inc(cv_pe, 1)

            pe.wait_ge(a_lo, 5)
            pe.wait_ge(cv_lo, 4)
            with pe.Fori(T_OUT // 4, T_FF0 // 4) as q:
                for s in range(4):
                    unit(q, s, h_hi, h_lo)

            def ff(layer, T0, nn, with_ada):
                J = 32 * layer
                q0 = T0 // 4

                def up(b, ada):
                    if ada:
                        for s in range(8):
                            ada_chunk(3 + b, s)
                            unit(q0 + 4 * b + s // 4, s % 4, h_hi, h_lo, from_norm(nn) if s == 0 else None)
                        ada_turn(3 + b)
                    else:
                        with pe.Fori(0, 2) as i:
                            for s in range(4):
                                unit(q0 + 4 * b + i, s, h_hi, h_lo, from_norm(nn) if s == 0 else None)

                def down(b):
                    def hid(k):
                        pe.wait_ge(hid_rdy, J + 8 * b + k + 1)
                    with pe.Fori(0, 2) as i:
                        for s in range(4):
                            unit(q0 + 4 * b + 2 + i, s, hid_hi, hid_lo, hid if s == 0 else None)

                with pe.Fori(0, 3) as b:
                    up(b, with_ada)
                    down(b)
                up(3, False)
                down(3)

            norm_stats(norm[1])
            ff(0, T_FF0, 1, True)
            norm_stats(norm[2])
            with pe.Fori(T_C // 4, T_OUTC // 4) as q:
                for s in range(4):
                    unit(q, s, h_hi, h_lo, from_norm(2) if s == 0 else None)

            pe.wait_ge(ws_in, 16)
            for g in range(8):
                ins = tr(ST[:, g // 4, 128 * (g % 4):128 * (g % 4) + 128], ws_raw[:, g, :], ident[:, :])
            ins.then_inc(w_pe, 1)
            pe.wait_ge(w_dve, 2)
            mm(AP[0:32, 0:32], rep4[:, :], ws_T[0:4, :, 0:4], start=True, stop=True).then_inc(w_pe, 1)

            def v_turn(tt):
                if tt >= 2:
                    pe.wait_ge(v_dve, tt - 1)
                if tt == 4:
                    pe.wait_ge(v_rows, 1)
                for ch in range(KC):
                    if tt < 4:
                        ins = tr(G[tt % 2][:, ch // 4, 128 * (ch % 4):128 * (ch % 4) + 128], tok(ab, 8 + ch, tt), ident[:, :])
                    else:
                        ins = tr(G[0][0:32, ch // 4, 128 * (ch % 4):128 * (ch % 4) + 128], v_smp[:, ch, :], ident[:, :])
                ins.then_inc(v_pe, 1)

            pe.wait_ge(psum_free, 2 + T_OUTC)
            v_turn(0)
            for tt in range(4):
                v_turn(tt + 1)
                pe.wait_ge(v_dve, tt + 1)
                for hb in range(2):
                    n = 2 * tt + hb
                    pe.wait_ge(g_d, 2 * n - 3) if n >= 2 else pe.wait_ge(w_dve, 3)
                    for g in range(4 * hb, 4 * hb + 4):
                        ins = mm(ST[:, n % 2, 128 * (g % 4):128 * (g % 4) + 128], vn[:, tt % 2, 128 * g:128 * g + 128],
                                 ws_T[:, g, :], start=True, stop=True)
                    ins.then_inc(g_pe, 1)
            pe.wait_ge(v_dve, 5)
            for g in range(8):
                ins = mm(AP[:, 32 * g:32 * g + 32], vns[:, 128 * g:128 * g + 128], ws_blk[:, g, :], start=True, stop=True)
            ins.then_inc(g_pe, 1)

            pe.wait_ge(g_lo, 9)
            with pe.Fori(T_OUTC // 4, T_FF1 // 4) as q:
                for s in range(4):
                    unit(q, s, h_hi, h_lo)
            norm_stats(norm[3])
            ff(1, T_FF1, 3, False)

            norm_stats(fin)
            pe.wait_ge(fin["y"], KC)
            pe.wait_ge(psum_free, 2 + T_END)
            for tt in range(5):
                if tt >= 2:
                    pe.wait_ge(fin["cp"], tt - 1)
                for ch in range(KC):
                    if tt < 4:
                        ins = tr(G[tt % 2][:, ch // 4, 128 * (ch % 4):128 * (ch % 4) + 128], tok(y_T, ch, tt), ident[:, :])
                    else:
                        ins = tr(G[0][0:32, ch // 4, 128 * (ch % 4):128 * (ch % 4) + 128], y_smp[:, ch, :], ident[:, :])
                ins.then_inc(fin["tp"], 1)


def kernel(x_prompt, x_sample, cache_k, cache_v, state_conv, page_table, c_prompt, c_sample, norm_g, w_ada, b_ada,
           w_in_ab, conv_w, w_out_ab, w_in_c, g_v, w_s, b_s, w_out_c, w_ff1, w_ff2, g_final):
    import numpy as _np
    import concourse.bacc as _bacc
    from concourse import mybir as _mybir
    from concourse.bass_utils import run_bass_kernel_spmd as _run

    f = _np.float32
    p = _np.arange(128)
    key = _np.arange(PAST)
    c = _np.arange(512)
    slope = _np.exp2(-8.0 * _np.arange(1, NH + 1) / NH)
    row_b, row_h, row_t = p // 32, p // 4 % 8, p % 4
    own = _np.arange(16)
    own_d = row_t[:, None] - own[None, :] % 4
    own_ok = (own[None, :] // 4 == row_b[:, None]) & (own_d >= 0)
    r32 = _np.arange(32)
    consts = {
        "k_ident": _np.eye(128),
        "k_dist": _np.where(c[None, :] - 384 <= p[:, None], c[None, :] - 384 - p[:, None], NEG),
        "k_head_mask": c[None, :] // HD == row_h[:, None],
        "k_own_bias": _np.where(own_ok, -own_d * slope[row_h][:, None] / SCALE, NEG),
        "k_past_bias": -(PAST + row_t[:, None] - key[None, :]) * slope[row_h][:, None] / SCALE,
        "k_slopes": _np.broadcast_to(slope / SCALE, (128, NH)),
        "k_rank4": _np.broadcast_to(_np.arange(1, 5), (128, 4)),
        "k_rep4": r32[None, :] % 4 == _np.arange(4)[:, None],
        "k_blk_mask": r32[:, None] // 4 == r32[None, :] // 4,
        "k_tri": p[:, None] <= p[None, :],
    }
    arrays = {n: _np.ascontiguousarray(v.astype(f)) for n, v in consts.items()}
    pt = _np.asarray(page_table).reshape(2, 4, 2, 4)
    k_order = pt.transpose(0, 2, 1, 3).reshape(2, 32)
    v_order = pt.reshape(2, 4, 8).transpose(0, 2, 1).reshape(2, 32)
    arrays["page_order"] = _np.ascontiguousarray(_np.concatenate([k_order, v_order], 1).reshape(1, 128))
    given = dict(x_prompt=x_prompt, x_sample=x_sample, cache_k=cache_k, cache_v=cache_v, state_conv=state_conv,
                 c_prompt=c_prompt, c_sample=c_sample, norm_g=norm_g, w_ada=w_ada, b_ada=b_ada, w_in_ab=w_in_ab,
                 conv_w=conv_w, w_out_ab=w_out_ab, w_in_c=w_in_c, g_v=g_v, w_s=w_s, b_s=b_s, w_out_c=w_out_c,
                 w_ff1=w_ff1, w_ff2=w_ff2, g_final=g_final)
    for n, v in given.items():
        arrays[n] = _np.ascontiguousarray(v)

    nc = _bacc.Bacc("TRN2", target_bir_lowering=False, num_devices=1)
    a = {n: nc.dram_tensor("in_" + n, v.shape, _mybir.dt.from_np(v.dtype), kind="ExternalInput").ap()
         for n, v in arrays.items()}
    shapes = [("y_prompt", (1, SEQ, D)), ("y_sample", (NB, NT, D)),
              ("k_prompt", (1, SEQ // PAGE, PAGE, NH, HD)), ("v_prompt", (1, SEQ // PAGE, PAGE, NH, HD)),
              ("conv_prompt", (1, 1, 2, D // 2)),
              ("k_sample", (1, NB, NT, NH, HD)), ("v_sample", (1, NB, NT, NH, HD)),
              ("conv_sample", (1, NB, 2, D // 2)), ("cv_sample", (1, NB, NT, D))]
    out = {n: nc.dram_tensor("out_" + n, s, _mybir.dt.float32, kind="ExternalOutput").ap() for n, s in shapes}
    trunk_kernel(nc, a, out)
    r = _run(nc, [{"in_" + n: v for n, v in arrays.items()}], core_ids=[0])
    return tuple(r.results[0]["out_" + n] for n, _ in shapes)
```

```python
import concourse.bass as bass
from concourse import mybir
from contextlib import ExitStack

import numpy as np

D = 1024
KC = D // 128
NH, HD = 8, 64
SEQ = 512
NB, NT = 8, 4
PAGE, NPAGES = 128, 8
PAST = PAGE * NPAGES
POOL_PAGES = 80
HALF = 256 + 16
LA = 3
WSLOTS = 4
EPS = 1e-6
SCALE = HD ** -0.5
NEG = -1e30

T_AB, T_OUT, T_FF0, T_C, T_OUTC, T_FF1, T_END = 0, 24, 32, 96, 112, 120, 184


def trunk_kernel(nc, a, out):
    f32, f32r, i32 = mybir.dt.float32, mybir.dt.float32r, mybir.dt.int32
    ALU = mybir.AluOpType
    ACT = mybir.ActivationFunctionType
    AX = mybir.AxisListType
    ds = bass.ds

    top = [16512]

    def place(name, shape, dt=f32, at=None):
        size = 4 * int(np.prod(shape[1:]))
        if at is None:
            at = top[0]
            top[0] += (size + 31) // 32 * 32
        return nc.alloc_sbuf_tensor_at(name, shape, dt, offset=at)

    raw = place("raw_panels", [128, 2, KC, 256])
    w_hi = place("w_hi", [128, WSLOTS, KC, 128], f32r)
    w_lo = place("w_lo", [128, WSLOTS, KC, 128], f32r)
    x = place("x_resid", [128, KC, 2, HALF])
    h_hi = place("h_hi", [128, KC, 2, HALF], f32r)
    h_lo = place("h_lo", [128, KC, 2, HALF], f32r)
    H0 = top[0] - 2 * 17408
    ada_h = place("ada_early_h", [128, 4, 2048], at=H0)
    y_all = place("y_tok", [128, 5, D], at=H0)
    A0 = top[0]
    ada_w = place("ada_w", [128, 2, 2048])
    kT = place("kT_pages", [128, 4, 4, 256], at=A0)
    pT = place("pT", [128, 8, 128], at=A0)
    k_tok = place("k_tok", [128, 4, 512], at=A0)
    C0 = A0 + 8192
    u_pad = place("u_pad", [128, 2 + SEQ], at=C0)
    u_smp = place("u_smp", [128, NB, 6], at=C0 + 2080)
    acc_cv = place("acc_cv", [128, 2, HALF], at=C0 + 2304)
    t_cv = place("t_cv", [128, 2, HALF], at=C0 + 4480)
    gv_row = place("gv_row", [128, D], at=A0)
    bs_row = place("bs_row", [128, 8, 128], at=A0 + 4096)
    ws_T = place("ws_T", [128, 8, 128], at=A0 + 8192)
    ws_blk = place("ws_blk", [32, 8, 32], at=A0 + 12288)
    gf_row = place("gf_row", [128, D], at=A0)
    B0 = top[0]
    V0 = B0 + 2 * 17408
    ab = place("ab", [128, 24, 2, HALF])
    x_tok = place("x_tok", [128, 4, D], at=B0)
    xs_tok = place("xs_tok", [32, D], at=B0 + 16384)
    hid_hi = place("hid_hi", [128, KC, 2, HALF], f32r, at=B0)
    hid_lo = place("hid_lo", [128, KC, 2, HALF], f32r, at=B0 + 17408)
    fin_junk = place("fin_junk", [128, 5, 128], at=V0)
    fin_ss = place("fin_ss", [128, KC, 5], at=V0 + 2560)
    x_smp = place("x_smp", [128, 2, 32], at=V0 + 2848)
    fin_r = place("fin_r", [128, 3, 5], at=V0 + 2752)
    v_T = place("v_T", [128, KC, 2, HALF], at=V0)
    junk = place("junk", [128, D], at=B0)
    v_smp = place("v_smp", [128, KC, 32], at=B0 + 4096)
    ws_raw = place("ws_raw", [128, 8, 128], at=V0)
    ident = place("ident", [128, 128])
    ones = place("ones", [128, 128])
    dist = place("dist", [128, 512])
    head_mask = place("head_mask", [128, 512])
    own_bias = place("own_bias", [128, 16])
    slopes = place("slopes", [128, NH])
    rank4 = place("rank4", [128, 4])
    rep4 = place("rep4", [4, 32])
    blk_mask = place("blk_mask", [32, 32])
    tri = place("tri", [128, 128])
    vec_rows = place("vec_rows", [128, 128], at=B0 + 24576)
    vec_rows2 = place("vec_rows2", [12, 128], at=B0 + 25088)
    vec = place("vec", [128, 140])
    pages_ix = place("pages_ix", [1, 128], i32)
    ada_b = place("ada_early_b", [128, 2, 2048], at=B0 + 26624)
    c_rows = place("c_rows", [9, D], at=B0 + 20480)
    cT = place("cT", [128, KC, 32])
    c_exp = place("c_exp", [128, KC, 9])
    c_tr = place("c_tr", [128, KC, 9])
    adaT = place("adaT", [128, 96, 9])
    amod = place("amod", [128, KC, 9])
    eps_t = place("eps", [128, 1])
    past_off = place("past_off", [128, 4])
    slope_row = place("slope_row", [128, 1])
    cv_state = place("cv_state", [128, 4, 18])
    st_T = place("st_T", [128, 4, 16])
    rtmp = place("rtmp", [128, 2, 16])
    S0 = top[0]
    sq = place("sq", [128, 2, 2, HALF], at=S0)
    hf = place("hf", [128, 2, 2, HALF], at=S0 + 4352)
    lnt = place("lnt", [128, 2, HALF], at=S0 + 8704)
    rstd = place("rstd", [128, 2, HALF], at=S0 + 10880)
    uu = place("uu", [128, 2, 2, HALF], at=S0 + 13056)
    rel = place("rel", [128, 2, 2, HALF], at=S0)
    ffv = place("ffv", [128, 2, HALF], at=S0 + 4352)
    ada_sb = place("ada_sb", [128, 512], at=S0 + 17408)
    ssq = place("ssq", [128, 2, HALF], at=S0 + 19456)
    kv_ring = place("kv_ring", [128, 8, 512], at=S0)
    s_sb = place("s_sb", [128, PAST + 16], at=S0 + 16384)
    k_own = place("k_own", [16, 2, 512], at=S0 + 16384)
    o_tmp = place("o_tmp", [128, 512], at=S0 + 16384)
    q_bd = place("q_bd", [128, 4, 128], at=S0 + 20544)
    pT_own = place("pT_own", [16, 128], at=S0 + 22592)
    o2 = place("o2", [128, 2, HD], at=S0 + 23104)
    sm = place("sm", [128, 32], at=S0 + 23616)
    v_own = place("v_own", [16, 2, 512], at=S0 + 23872)
    k_row = place("k_row", [128, 256], at=S0 + 27968)
    assert S0 + 28992 <= 229344, S0
    dist_h = place("dist_h", [128, 512], at=S0)
    P = place("P", [128, 2, 1280], at=S0 + 2048)
    PT = place("PT", [128, 1280], at=S0 + 12288)
    v_tok = place("v_tok", [128, 4, 512], at=S0 + 17408)
    pm = place("pm", [128, 2, 16], at=S0 + 25600)
    st_rows = place("st_rows", [16, 512], at=B0 + 14 * 2176)
    cv_out = place("cv_out", [18, 512], at=S0 + 25728)
    vn = place("vn", [128, 4, D], at=S0)
    vns = place("vns", [32, D], at=S0 + 16384)
    gate_s = place("gate_s", [128, 2, 2, HALF], at=S0 + 20480)
    gated = place("gated", [128, 2, HALF], at=S0 + 24832)
    vst = place("vst", [128, 3, 5], at=S0 + 27008)

    ctx = ExitStack()
    with ctx:
        G = [ctx.enter_context(nc.psum_tensor(f"gemm{i}", [128, 2, 512], f32)) for i in range(2)]
        XA = ctx.enter_context(nc.psum_tensor("aux_ps", [128, 2, 512], f32))
        ST = ctx.enter_context(nc.psum_tensor("stat_ps", [128, 2, 512], f32))
        AP, TP = XA[:, 0, :], XA[:, 1, :]

        def sem(name):
            return ctx.enter_context(nc.semaphore(name))

        raw_in = [sem("raw_in0"), sem("raw_in1")]
        hi_done, lo_done = sem("hi_done"), sem("lo_done")
        unit_done = sem("unit_done")
        psum_free = sem("psum_free")
        res_tmp, relu_r, relu_hi, hid_rdy = sem("res_tmp"), sem("relu_r"), sem("relu_hi"), sem("hid_rdy")
        ada0_in = [sem(f"ada0_in{k}") for k in range(KC)]
        ada_in = [sem("ada_in0"), sem("ada_in1")]
        ada_used, ada_copied, ada_tp, ada_T = sem("ada_used"), sem("ada_copied"), sem("ada_tp"), sem("ada_T")
        c_in, vec_in, const_in, x_in = sem("c_in"), sem("vec_in"), sem("const_in"), sem("x_in")
        pe_c, pe_vec, act_c, dve_c, dve_init, dve_vec = (sem("pe_c"), sem("pe_vec"), sem("act_c"), sem("dve_c"),
                                                        sem("dve_init"), sem("dve_vec"))
        pe_x, x_cp, x_cs = sem("pe_x"), sem("x_cp"), sem("x_cs")
        norm = [{k: sem(f"norm{n}_{k}") for k in ("mod", "sq", "acc", "st", "rs", "u", "s1", "s2", "hf", "hi", "h")}
                for n in range(4)]
        fin = {k: sem(f"fin_{k}") for k in ("zero", "g", "smp", "tp", "sq", "rs", "y")}
        out_done = sem("out_done")
        y_out = sem("y_out")
        tma_pe, tma_ev = sem("tma_pe"), sem("tma_ev")
        tmb_pe, tmb_ev = sem("tmb_pe"), sem("tmb_ev")
        st_in, gm_in, ws_in = sem("st_in"), sem("gm_in"), sem("ws_in")
        pg_in = [sem(f"pg_in{i}") for i in range(8)]
        page_free = sem("page_free")
        qz, q_rdy, kt_act, kt_dve, s_pe = sem("q_zero"), sem("q_rdy"), sem("kt_act"), sem("kt_dve"), sem("s_pe")
        sd, s_exp, p_pe, p_act, o2_pe = sem("s_dve"), sem("s_exp"), sem("p_pe"), sem("p_act"), sem("o2_pe")
        a_s, a_max, a_nrm, a_exp, a_tp, a_ev, a_ev2, a_o, a_out, mix_hi, mix_rdy = (sem(n) for n in (
            "att_scores", "att_maxima", "att_normalised", "att_exp", "att_tp", "att_ev", "att_ev_dve", "att_o", "att_out",
            "mix_hi", "mix_rdy"))
        cv, cv_pe, cv_ev = sem("conv_pool"), sem("conv_pe"), sem("conv_ev")
        w_pe, w_dve, v_rows, v_pe, v_act, v_dve, g_pe, g_s, g_hi, g_lo = (sem(n) for n in (
            "ws_pe", "ws_dve", "v_rows", "v_pe", "v_act", "v_dve", "g_pe", "gate_s_rdy", "g_hi", "g_lo"))

        panel = {"in_ab": a["w_in_ab"][0].rearrange("(k p) n -> p k n", p=128),
                 "out_ab": a["w_out_ab"][0].rearrange("(k p) n -> p k n", p=128),
                 "in_c": a["w_in_c"][0].rearrange("(k p) n -> p k n", p=128),
                 "out_c": a["w_out_c"][0].rearrange("(k p) n -> p k n", p=128)}
        ff1_v = [a["w_ff1"][l].rearrange("(k p) n -> p k n", p=128) for l in range(2)]
        ff2_v = [a["w_ff2"][l].rearrange("(k p) n -> p k n", p=128) for l in range(2)]
        gp = [G[s][:, :, 0:256] for s in range(2)]
        gs = [G[s][:, :, 256:272] for s in range(2)]
        BANKS = [G[0][:, 0, :], G[0][:, 1, :], G[1][:, 0, :], G[1][:, 1, :]]

        def bt(ap):
            return ap.rearrange("p h (b t) -> p h b t", t=NT)

        def per_row(rows):
            return rows.rearrange("p (h b) -> p h b", h=2).unsqueeze(3).broadcast_to([128, 2, 4, NT])

        def tok(buf, c, tt):
            return buf[:, c, tt // 2, 128 * (tt % 2):128 * (tt % 2) + 128]

        QOFF = [0, 128, 384, 768]

        VB = [XA[:, :, :], ST[:, :, :]]
        SCB = [BANKS[2][:, 0:128], BANKS[3][:, 0:256], BANKS[2][:, 128:512], AP]
        PTO = [0, 512, 896, 1152]
        PTB = [TP, ST[:, 0, 0:384], BANKS[3][:, 256:512], ST[:, 0, 384:512]]
        OUTB = ST[:, 1, :]
        KTB = [BANKS[2], BANKS[3], TP]
        PTT = [TP, BANKS[2], BANKS[3]]
        TMA = [AP, TP, ST[:, 0, :], ST[:, 1, :]]
        TMB = [BANKS[2], BANKS[3], ST[:, 0, :], ST[:, 1, :], TP, ST[:, 0, :], ST[:, 1, :], TP]
        TMB_USED = {5: 3, 6: 4, 7: 5}
        SD_EXP, SD_P, SD_O2, SD_STEPS = 17, 19, 22, 30
        SD0 = UD0 = HR0 = 1
        MAX_STEPS, NRM_STEPS = 6, 5
        HALF_AT = {0: 2, 1: 3, 2: 4, 3: 5, 5: 6, 6: 7}
        CV_STEPS = 14
        N_STORES = 2 + 2 + 4 + 4 + 2 + 1
        N_CONST = 12
        ADA0 = [ada_w[:, 0, :], ada_w[:, 1, :]] + [ada_h[:, i, :] for i in range(4)] + [ada_b[:, i, :] for i in range(2)]
        KV_OUT = 4
        MIX = [0, 1, 4, 2, 5, 6, 7, 3]

        def mix_src(c):
            return ab[:, c, :, :] if c < 4 else ab[:, 8 + c, :, :]

        block = ctx.enter_context(nc.Block())

        @block.sync
        def _(sp):
            sp.dma_start(c_rows[0:1, :], a["c_prompt"]).then_inc(c_in, 16)
            sp.dma_start(c_rows[1:9, :], a["c_sample"]).then_inc(c_in, 16)
            sp.dma_start(ident[:, :], a["k_ident"]).then_inc(c_in, 16)
            for tt in range(4):
                sp.dma_start(x_tok[:, tt, :], a["x_prompt"][0, 128 * tt:128 * tt + 128, :]).then_inc(x_in, 16)
            sp.dma_start(xs_tok[:, :], a["x_sample"].rearrange("b t n -> (b t) n")).then_inc(x_in, 16)
            sp.dma_start(vec_rows[0:96, :], a["b_ada"].rearrange("l (c n) -> (l c) n", n=128)).then_inc(vec_in, 16)
            sp.dma_start(vec_rows[96:128, :], a["norm_g"].rearrange("l s (c n) -> (l s c) n", n=128)).then_inc(vec_in, 16)
            sp.dma_start(vec_rows2[:, :], a["conv_w"].rearrange("l w (c n) -> (l w c) n", n=128)).then_inc(vec_in, 16)

            def load_panel(p, slot, src, wait=True):
                if wait:
                    sp.wait_ge(lo_done, 2 * p - 2)
                sp.dma_start(raw[:, slot, :, :], src).then_inc(raw_in[slot], 16)

            def two_panels(p, view, col, rows=None):
                for s in range(2):
                    src = view[:, :, ds(col + 256 * s, 256)] if rows is None else view[:, ds(rows, KC), ds(col + 256 * s, 256)]
                    load_panel(p + s, s, src)

            load_panel(0, 0, panel["in_ab"][:, :, 0:256], wait=False)
            sp.wait_ge(ada0_in[6], 16)
            load_panel(1, 1, panel["in_ab"][:, :, 256:512], wait=False)
            for dst, src in ((dist, "k_dist"), (head_mask, "k_head_mask"), (own_bias, "k_own_bias"), (slopes, "k_slopes"),
                             (rank4, "k_rank4"), (k_row, "k_row"), (past_off, "k_past_off"),
                             (slope_row, "k_slope_row"), (rep4, "k_rep4"), (blk_mask, "k_blk_mask"), (tri, "k_tri"),
                             (pages_ix, "page_order")):
                sp.dma_start(dst[:, :], a[src]).then_inc(const_in, 16)
            with sp.Fori(1, 3) as i:
                two_panels(2 * i, panel["in_ab"], 512 * i)
            two_panels(6, panel["in_ab"], 2048)
            sp.wait_ge(const_in, 16 * N_CONST)
            sp.wait_ge(norm[0]["h"], KC)

            def load_pages(m0, cache):
                _, page = nc.values_load_multi_w_load_instructions(pages_ix[0:1, ds(m0, 8)], engines=(mybir.EngineType.SP,),
                                                                   min_val=0, max_val=POOL_PAGES - 1)
                for s in range(8):
                    sp.wait_ge(page_free, m0 + s + 1)
                    sp.dma_start(kv_ring[:, s, :],
                                 a[cache][0].rearrange("a p h d -> a p (h d)")[ds(page[s], 1), :, :]
                                 .rearrange("a p n -> (a p) n")).then_inc(pg_in[s], 16)

            with sp.Fori(0, 2) as g:
                for quarter in range(4):
                    load_pages(64 * g + 8 * quarter, "cache_k")
                load_pages(64 * g + 32, "cache_v")
                load_panel(8 + 2 * g, 0, panel["in_ab"][:, :, ds(g * (-1024) + 2560, 256)])
                load_panel(9 + 2 * g, 1, panel["in_ab"][:, :, ds(g * (-1024) + 2816, 256)])
                with sp.Fori(1, 4) as q:
                    load_pages(64 * g + 32 + 8 * q, "cache_v")
            two_panels(12, panel["out_ab"], 0)
            two_panels(14, panel["out_ab"], 512)

            def load_ff(layer, p0):
                with sp.Fori(0, 4) as b:
                    with sp.Fori(0, 2) as i:
                        two_panels(p0 + 8 * b + 2 * i, ff1_v[layer], 1024 * b + 512 * i)
                    with sp.Fori(0, 2) as i:
                        two_panels(p0 + 8 * b + 4 + 2 * i, ff2_v[layer], 512 * i, rows=KC * b)

            load_ff(0, T_FF0 // 2)
            for part, col in ((0, D), (4, 0)):
                with sp.Fori(0, 2) as i:
                    two_panels(T_C // 2 + part + 2 * i, panel["in_c"], col + 512 * i)
            with sp.Fori(0, 2) as i:
                two_panels(T_OUTC // 2 + 2 * i, panel["out_c"], 512 * i)
            load_ff(1, T_FF1 // 2)

            for tt in range(4):
                sp.wait_ge(fin["y"], tt + 1)
                sp.dma_start(out["y_prompt"][0, 128 * tt:128 * tt + 128, :], y_all[:, tt, :]).then_inc(y_out, 16)
            sp.wait_ge(fin["y"], 5)
            sp.dma_start(out["y_sample"].rearrange("b t n -> (b t) n"), y_all[0:32, 4, :]).then_inc(y_out, 16)
            sp.wait_ge(y_out, 80)
            sp.wait_ge(out_done, 16 * N_STORES)

        @block.gpsimd
        def _(pool):
            def load_ada(c, slot, src):
                pool.wait_ge(ada_used, c - 1)
                pool.dma_start(ada_w[:, slot, :], src).then_inc(ada_in[slot], 16)

            ada_v = [a["w_ada"][l].rearrange("(k p) (g n) -> g p k n", p=128, n=2048) for l in range(2)]
            def add_squares(s, m):
                pool.wait_ge(s["sq"], m + 1)
                if m > 1:
                    pool.wait_ge(s["acc"], m - 1)
                nc.gpsimd.tensor_tensor(ssq[:, :, :], ssq[:, :, :], sq[:, m % 2, :, :], ALU.add).then_inc(s["acc"], 1)

            def norm_apply(nn):
                s = norm[nn]
                base = 48 * (nn // 2) + (0 if nn % 2 == 0 else 24)
                for c in range(KC):
                    pool.wait_ge(s["u"], c + 1)
                    if c >= 2:
                        pool.wait_ge(s["h"], c - 1)
                        pool.wait_ge(s["hi"], c - 1)
                    nc.gpsimd.tensor_tensor(bt(hf[:, c % 2, :, 256:272]), bt(uu[:, c % 2, :, 256:272]),
                                            per_row(amod[:, c, 1:9]), ALU.mult).then_inc(s["s1"], 1)
                    pool.wait_ge(s["s1"], c + 1)
                    nc.gpsimd.tensor_tensor(bt(hf[:, c % 2, :, 256:272]), bt(hf[:, c % 2, :, 256:272]),
                                            per_row(adaT[:, base + c, 1:9]), ALU.add).then_inc(s["s2"], 1)

            pool.wait_ge(c_in, 48)
            for k in range(KC):
                pool.dma_start(ADA0[k], ada_v[0][0, :, k, :]).then_inc(ada0_in[k], 16)
            for m in range(1, 7):
                add_squares(norm[0], m)
            for c in (8, 9):
                load_ada(c, c % 2, ada_v[0][1, :, c % 8, :])
            norm_apply(0)
            with pool.Fori(1, 4) as j:
                for s in range(2):
                    load_ada(8 + 2 * j + s, s, ada_v[0][1, :, ds(2 * j + s, 1), :])

            for g in range(2):
                pool.wait_ge(tma_ev, g + 1)
                pool.dma_start(out["v_sample"][0, 4 * g:4 * g + 4].rearrange("b t h d -> (b t) (h d)"),
                               v_own[:, g, :]).then_inc(out_done, 16)
            for g in range(2):
                pool.wait_ge(tma_ev, g + 3)
                pool.dma_start(out["k_sample"][0, 4 * g:4 * g + 4].rearrange("b t h d -> (b t) (h d)"),
                               k_own[:, g, :]).then_inc(out_done, 16)

            pool.dma_start(st_rows[:, :], a["state_conv"][0].rearrange("b r n -> (b r) n")).then_inc(st_in, 16)
            for tt in range(4):
                pool.wait_ge(tmb_ev, tt + 1)
                pool.dma_start(out["k_prompt"][0, tt].rearrange("p h d -> p (h d)"), k_tok[:, tt, :]).then_inc(out_done, 16)
            for tt in range(4):
                pool.wait_ge(tmb_ev, tt + 5)
                pool.dma_start(out["v_prompt"][0, tt].rearrange("p h d -> p (h d)"), v_tok[:, tt, :]).then_inc(out_done, 16)
            pool.wait_ge(cv_ev, 1)
            n = [0]

            def did(ins):
                n[0] += 1
                ins.then_inc(cv, 1)

            def after():
                pool.wait_ge(cv, n[0])

            def smp(ap):
                return ap.rearrange("p (h b) t -> p h b t", h=2)

            for ch in range(4):
                cw = [vec[:, 128 + 4 * i + ch:129 + 4 * i + ch] for i in range(3)]
                if ch:
                    after()
                did(nc.gpsimd.memset(u_pad[:, 0:2], 0.0))
                did(nc.gpsimd.tensor_tensor(u_pad[:, 2:].rearrange("p (h n) -> p h n", h=2), ab[:, 16 + ch, :, 0:256],
                                            ab[:, 20 + ch, :, 0:256], ALU.mult))
                did(nc.gpsimd.tensor_copy(u_smp[:, :, 0:2], st_T[:, ch, :].rearrange("p (b r) -> p b r", r=2)))
                did(nc.gpsimd.tensor_tensor(smp(u_smp[:, :, 2:6]), bt(ab[:, 16 + ch, :, 256:272]),
                                            bt(ab[:, 20 + ch, :, 256:272]), ALU.mult))
                after()
                for i in range(3):
                    dst = acc_cv if i == 0 else t_cv
                    did(nc.gpsimd.tensor_scalar(dst[:, :, 0:256], u_pad[:, i:i + SEQ].rearrange("p (h n) -> p h n", h=2),
                                                cw[i], None, ALU.mult))
                    did(nc.gpsimd.tensor_scalar(bt(dst[:, :, 256:272]), smp(u_smp[:, :, i:i + 4]), cw[i], None, ALU.mult))
                    after()
                    if i:
                        dst = acc_cv[:, :, :] if i == 1 else ab[:, 16 + ch, :, :]
                        did(nc.gpsimd.tensor_tensor(dst, acc_cv[:, :, :], t_cv[:, :, :], ALU.add))
                        after()
                did(nc.gpsimd.tensor_copy(cv_state[:, ch, 0:16].rearrange("p (b r) -> p b r", r=2), u_smp[:, :, 4:6]))
                did(nc.gpsimd.tensor_copy(cv_state[:, ch, 16:18], u_pad[:, SEQ:SEQ + 2]))
                assert n[0] == CV_STEPS * (ch + 1)

            pool.wait_ge(cv, 4 * CV_STEPS)
            pool.wait_ge(out_done, 16 * 12)
            for c in (16, 17):
                load_ada(c, c % 2, ada_v[0][2, :, c % 8, :])
            for ch in range(4):
                pool.wait_ge(psum_free, 2 + 21 + ch)
                did(nc.gpsimd.tensor_tensor(ab[:, 12 + ch, :, :], ab[:, 16 + ch, :, :], ab[:, 12 + ch, :, :], ALU.mult))
            pool.wait_ge(cv_ev, 2)
            pool.dma_start(out["conv_sample"][0].rearrange("b r n -> (b r) n"), cv_out[0:16, :]).then_inc(out_done, 16)
            pool.dma_start(out["conv_prompt"][0, 0], cv_out[16:18, :]).then_inc(out_done, 16)
            for m in range(KC):
                if m < 6:
                    load_ada(18 + m, m % 2, ada_v[0][2, :, 2 + m, :])
                if 1 <= m <= 6:
                    add_squares(norm[1], m)
            for c in range(2):
                load_ada(24 + c, c, ada_v[1][0, :, c, :])
            norm_apply(1)
            with pool.Fori(1, 4) as j:
                for s in range(2):
                    load_ada(24 + 2 * j + s, s, ada_v[1][0, :, ds(2 * j + s, 1), :])
            with pool.Fori(1, 3) as g:
                with pool.Fori(0, 4) as j:
                    for s in range(2):
                        load_ada(24 + 8 * g + 2 * j + s, s, ada_v[1][ds(g, 1), :, ds(2 * j + s, 1), :])

            pool.wait_ge(ada_used, 48)
            pool.dma_start(ws_raw[:, :, :], a["w_s"][0].rearrange("g t s -> t g s")).then_inc(ws_in, 16)
            pool.dma_start(gv_row[:, :], a["g_v"].broadcast_to([128, D])).then_inc(gm_in, 16)
            pool.dma_start(bs_row[:, :, :].rearrange("p g t -> p (g t)"),
                           a["b_s"].rearrange("l g t -> l (g t)").broadcast_to([128, D])).then_inc(gm_in, 16)
            for m in range(1, 7):
                add_squares(norm[2], m)
            norm_apply(2)
            pool.wait_ge(v_dve, 5)
            pool.dma_start(out["cv_sample"][0].rearrange("b t n -> (b t) n"), vns[:, :]).then_inc(out_done, 16)
            for m in range(1, 7):
                add_squares(norm[3], m)
            norm_apply(3)
            pool.wait_ge(v_dve, 5)
            pool.dma_start(gf_row[:, :], a["g_final"].rearrange("(a n) -> a n", a=1).broadcast_to([128, D])).then_inc(fin["g"], 16)
            for c in range(KC):
                pool.wait_ge(psum_free, 2 + T_END - KC + c + 1)
                if c >= 2:
                    pool.wait_ge(fin["tp"], c - 1)
                nc.gpsimd.tensor_copy(x_smp[:, c % 2, :].rearrange("p (h n) -> p h n", h=2),
                                      x[:, c, :, 256:272]).then_inc(fin["smp"], 1)

        @block.scalar
        def _(act):
            A = nc.scalar.activation

            def split_hi(u):
                q, s = u
                act.wait_ge(raw_in[(s // 2) % 2], 16 * q + 16)
                if not (isinstance(q, int) and 4 * q + s < 4):
                    act.wait_ge(unit_done, UD0 + 4 * q + s - 3)
                A(w_hi[:, s, :, :], raw[:, (s // 2) % 2, :, 128 * (s % 2):128 * (s % 2) + 128], ACT.Copy).then_inc(hi_done, 1)

            def ahead(q, s):
                return (q + (s + LA) // 4, (s + LA) % 4)

            def step_copy(q, s, idx, dst=None):
                t = 4 * q + s
                split_hi(ahead(q, s))
                copy_out(t, s % 2, ab if dst is None else dst, idx)

            def copy_out(t, slot, dst, idx):
                act.wait_ge(unit_done, UD0 + t + 1)
                A(dst[:, ds(idx, 1), :, :], G[slot][:, :, 0:HALF].unsqueeze(1), ACT.Copy).then_inc(psum_free, 1)

            def step_relu(q, s, j, m):
                t = 4 * q + s
                split_hi(ahead(q, s))
                act.wait_ge(unit_done, UD0 + t + 1)
                act.wait_ge(psum_free, t + 1)
                A(rel[:, s % 2, :, :], G[s % 2][:, :, 0:HALF], ACT.Relu).then_inc(relu_r, 1)
                act.wait_ge(relu_r, j + 1)
                A(hid_hi[:, ds(m, 1), :, :], rel[:, s % 2, :, :].unsqueeze(1), ACT.Square).then_inc(relu_hi, 1)

            def step_none(q, s):
                split_hi(ahead(q, s))

            def ada_copy(g):
                act.wait_ge(ada_used, 8 * g + 8)
                act.wait_ge(ada_tp, g)
                A(ada_sb[:, :], AP[:, :], ACT.Copy).then_inc(ada_copied, 1)

            def square(s, m):
                if m == 0:
                    A(ssq[:, :, :], x[:, m, :, :], ACT.Square).then_inc(s["sq"], 1)
                    return
                if m >= 3:
                    act.wait_ge(s["acc"], m - 2)
                A(sq[:, m % 2, :, :], x[:, m, :, :], ACT.Square).then_inc(s["sq"], 1)

            def norm_rstd(s):
                act.wait_ge(s["st"], 1)
                A(lnt[:, :, :], ST[:, :, 0:HALF], ACT.Ln, bias=eps_t[:, 0:1], scale=1.0 / D).then_inc(s["rs"], 1)
                act.wait_ge(s["rs"], 1)
                A(rstd[:, :, :], lnt[:, :, :], ACT.Exp, scale=-0.5).then_inc(s["rs"], 1)

            def resid_and_squares(T, s, at=None):
                for m in range(KC):
                    t = T + m
                    if at and m in at:
                        at[m]()
                    step_none(t // 4, t % 4)
                    if m >= 1:
                        act.wait_ge(psum_free, 2 + t)
                        square(s, m - 1)
                act.wait_ge(psum_free, 2 + T + KC)
                square(s, KC - 1)

            def norm_apply(nn, between=None):
                s = norm[nn]
                sh = 48 * (nn // 2) + (0 if nn % 2 == 0 else 24)
                for c in range(KC):
                    act.wait_ge(s["u"], c + 1)
                    if c >= 2:
                        act.wait_ge(s["h"], c - 1)
                    A(hf[:, c % 2, :, 0:256], uu[:, c % 2, :, 0:256], ACT.Identity,
                      bias=adaT[:, sh + c, 0:1], scale=amod[:, c, 0:1]).then_inc(s["hf"], 1)
                    act.wait_ge(s["hf"], c + 1)
                    act.wait_ge(s["s2"], c + 1)
                    A(h_hi[:, c, :, :], hf[:, c % 2, :, :], ACT.Copy).then_inc(s["hi"], 1)
                    if between and c == 5:
                        between()

            act.preload_act_table_set("natural_log_exp_and_others")
            act.wait_ge(pe_c, 1)
            act.wait_ge(dve_init, 3)
            A(c_exp[:, :, :], AP[:, 0:72].rearrange("p (k r) -> p k r", r=9), ACT.Exp, scale=-1.0).then_inc(act_c, 1)
            A(c_tr[:, :, :], AP[:, 0:72].rearrange("p (k r) -> p k r", r=9), ACT.Copy).then_inc(act_c, 1)
            for c in range(KC):
                act.wait_ge(pe_x, c + 1)
                A(x[:, c, :, 256:272], G[c % 2][:, 1, 0:32].rearrange("p (h n) -> p h n", h=2), ACT.Copy).then_inc(x_cs, 1)
            for c in range(KC):
                act.wait_ge(x_cp, c + 1)
                act.wait_ge(x_cs, c + 1)
                square(norm[0], c)
            split_hi((0, 0))
            split_hi((0, 1))
            norm_rstd(norm[0])
            ada_copy(0)
            norm_apply(0, lambda: split_hi((0, 2)))

            for t in range(12):
                if t == 9:
                    ada_copy(1)
                step_copy(t // 4, t % 4, t)

            for i in range(4):
                act.wait_ge(tma_pe, i + 1)
                dst = v_own if i < 2 else k_own
                A(dst[:, i % 2, :], TMA[i][0:16, :], ACT.Copy).then_inc(tma_ev, 1)

            with act.Fori(0, 2) as g:
                for quarter in range(4):
                    for n in range(8 * quarter, 8 * quarter + 8, 2):
                        b, pg = n // 2 % 4, n % 2
                        act.wait_ge(page_free, 64 * g + 8 + n + 1)
                        act.wait_ge(s_pe, 4 * g + quarter) if quarter else None
                        A(kT[:, :, b, 128 * pg:128 * pg + 128], KTB[n % 3].rearrange("p (r n) -> p r n", r=4),
                          ACT.Copy).then_inc(kt_act, 1)
                    if quarter == 1:
                        split_hi(ahead(3 + g, 0))
                act.wait_ge(sd, SD0 + SD_STEPS * g + SD_EXP)
                A(s_sb[:, :], s_sb[:, :], ACT.Exp, bias=sm[:, 9:10], scale=SCALE, accum_out=sm[:, 10:11]).then_inc(s_exp, 1)
                copy_out(12 + 4 * g, 0, ab, 16 + 4 * g)
                for n in range(9):
                    act.wait_ge(p_pe, 9 * g + n + 1)
                    if n < 8:
                        A(pT[:, n, :], PTT[n % 3][:, 0:128], ACT.Copy).then_inc(p_act, 1)
                    else:
                        A(pT_own[:, :], PTT[n % 3][0:16, 0:128], ACT.Copy).then_inc(p_act, 1)
                for s in range(1, 4):
                    split_hi(ahead(3 + g, s))
                    copy_out(12 + 4 * g + s, 0, ab, 16 + 4 * g + s)

            for i in range(8):
                if i == 4:
                    act.wait_ge(cv_pe, 1)
                    A(st_T[:, :, :].rearrange("p c r -> p (c r)"), AP[:, 0:64], ACT.Copy).then_inc(cv_ev, 1)
                act.wait_ge(tmb_pe, i + 1)
                dst = k_tok if i < 4 else v_tok
                A(dst[:, i % 4, :], TMB[i], ACT.Copy).then_inc(tmb_ev, 1)

            def exps(h):
                act.wait_ge(a_max, MAX_STEPS * (h + 1))
                for i in range(4):
                    sl = P[:, h % 2, QOFF[i]:QOFF[i] + 128 * (i + 1)]
                    A(sl, sl, ACT.Exp, bias=pm[:, h % 2, 4 + i:5 + i], scale=SCALE,
                      accum_out=pm[:, h % 2, 8 + i:9 + i]).then_inc(a_exp, 1)

            def mix(n0, n1):
                for c in MIX[n0:n1]:
                    if c >= 4:
                        act.wait_ge(cv, 4 * CV_STEPS + c - 3)
                    else:
                        act.wait_ge(a_out, c + 1)
                    A(h_hi[:, c, :, :], mix_src(c), ACT.Copy).then_inc(mix_hi, 1)

            exps(0)
            split_hi(ahead(5, 0))
            for h in range(NH):
                if h + 1 < NH:
                    exps(h + 1)
                if h % 2 == 0 and h < 6:
                    copy_out(20 + h // 2, 0, ab, 12 + h // 2)
                for n, j in enumerate((2, 0)):
                    act.wait_ge(a_tp, 4 * h + 3 + n)
                    if h:
                        act.wait_ge(a_o, h)
                    A(PT[:, PTO[j]:PTO[j] + 512 - 128 * j], PTB[j][:, 0:512 - 128 * j], ACT.Copy).then_inc(a_ev, 1)
                if h == 6:
                    copy_out(23, 0, ab, 15)
                if h % 2 and h < NH - 1:
                    split_hi(ahead(5, (h + 1) // 2))
                if h == NH - 1:
                    mix(0, 3)
                if h % 2:
                    act.wait_ge(a_o, h + 1)
                    A(ab[:, h // 2, :, 0:256], OUTB.rearrange("p (h n) -> p h n", h=2), ACT.Copy).then_inc(a_out, 1)
            mix(3, KC)
            act.wait_ge(cv_pe, 2)
            A(cv_out[:, :], TP[0:18, :], ACT.Copy).then_inc(cv_ev, 1)

            act.wait_ge(out_done, 16 * 12)
            resid_and_squares(T_OUT, norm[1], at={7: lambda: ada_copy(2)})

            def token_chunk(c):
                act.wait_ge(fin["tp"], c + 1)
                A(y_all[:, 0:4, 128 * c:128 * c + 128], VB[c % 2][:, 0, :].rearrange("p (t n) -> p t n", t=4), ACT.Copy)
                A(y_all[0:32, 4, 128 * c:128 * c + 128], VB[c % 2][0:32, 1, 0:128], ACT.Copy)
                if c:
                    act.wait_ge(fin["sq"], c)
                for tt in range(5):
                    m = 128 if tt < 4 else 32
                    src = VB[c % 2][:, 0, 128 * tt:128 * tt + 128] if tt < 4 else VB[c % 2][0:32, 1, 0:128]
                    ins = A(fin_junk[0:m, tt, :], src, ACT.Square, scale=D ** -0.5, accum_out=fin_ss[0:m, c, tt:tt + 1])
                ins.then_inc(fin["sq"], 1)

            def ff(layer, T0, s_next=None):
                J = 32 * layer
                q0 = T0 // 4

                def up(b, ada):
                    for s in range(8):
                        if s == 7 and ada:
                            ada_copy(3 + b)
                        step_relu(q0 + 4 * b + s // 4, s % 4, J + 8 * b + s, s)

                def up_short(b):
                    with act.Fori(0, 2) as i:
                        for s in range(4):
                            step_relu(q0 + 4 * b + i, s, J + 8 * b + 4 * i + s, 4 * i + s)

                def down(b):
                    with act.Fori(0, 2) as i:
                        for s in range(4):
                            step_none(q0 + 4 * b + 2 + i, s)

                ada = layer == 0
                up(0, ada)
                down(0)
                with act.Fori(1, 3) as b:
                    up(b, True) if ada else up_short(b)
                    down(b)
                up_short(3)
                if layer == 0:
                    resid_and_squares(T0 + 56, s_next)
                    return
                act.wait_ge(fin["zero"], 1)
                for m in range(KC):
                    t = T0 + 56 + m
                    if t + LA < T_END:
                        step_none(t // 4, t % 4)
                    if m >= 1:
                        token_chunk(m - 1)
                token_chunk(KC - 1)

            norm_rstd(norm[1])
            norm_apply(1)
            ff(0, T_FF0, norm[2])
            norm_rstd(norm[2])
            norm_apply(2)
            for t in range(T_C, T_C + 8):
                step_copy(t // 4, t % 4, t - T_C, dst=v_T)

            act.wait_ge(psum_free, 2 + T_C + 8)
            A(v_smp[:, :, :].rearrange("p c (h n) -> p c h n", h=2), v_T[:, :, :, 256:272], ACT.Copy).then_inc(v_rows, 1)

            def v_rms(tt):
                m = 128 if tt < 4 else 32
                act.wait_ge(v_pe, tt + 1)
                if tt:
                    act.wait_ge(v_act, 3 * tt)
                A(junk[0:m, :], VB[tt % 2][0:m, :, :].rearrange("p a n -> p (a n)"), ACT.Square,
                  accum_out=vst[0:m, 0, tt:tt + 1]).then_inc(v_act, 1)
                act.wait_ge(v_act, 3 * tt + 1)
                A(vst[0:m, 1, tt:tt + 1], vst[0:m, 0, tt:tt + 1], ACT.Ln, bias=eps_t[0:m, 0:1], scale=1.0 / D).then_inc(v_act, 1)
                act.wait_ge(v_act, 3 * tt + 2)
                A(vst[0:m, 2, tt:tt + 1], vst[0:m, 1, tt:tt + 1], ACT.Exp, scale=-0.5).then_inc(v_act, 1)

            for tt in (0, 1):
                v_rms(tt)
            step_none((T_C + 8) // 4, 0)
            for tt in (2, 3, 4):
                v_rms(tt)
            for m in range(8):
                if m:
                    step_none((T_C + 8 + m) // 4, m % 4)
                act.wait_ge(psum_free, 2 + T_C + 8 + m + 1)
                A(hid_hi[:, m, :, :], gated[:, :, :], ACT.Copy).then_inc(g_hi, 1)

            act.wait_ge(out_done, 16 * N_STORES)
            resid_and_squares(T_OUTC, norm[3])
            norm_rstd(norm[3])
            norm_apply(3)
            ff(1, T_FF1)

            act.wait_ge(fin["rs"], 1)
            A(fin_r[:, 1, :], fin_r[:, 0, :], ACT.Ln, bias=eps_t[:, 0:1]).then_inc(fin["rs"], 1)
            act.wait_ge(fin["rs"], 2)
            A(fin_r[:, 2, :], fin_r[:, 1, :], ACT.Exp, scale=-0.5).then_inc(fin["rs"], 1)

        @block.vector
        def _(dve):
            V = nc.vector

            def split_lo(u):
                q, s = u
                dve.wait_ge(hi_done, 4 * q + s + 1)
                V.tensor_tensor(w_lo[:, s, :, :], raw[:, (s // 2) % 2, :, 128 * (s % 2):128 * (s % 2) + 128],
                                w_hi[:, s, :, :].bitcast(f32), ALU.subtract).then_inc(lo_done, 1)

            def ahead(q, s):
                return (q + (s + LA) // 4, (s + LA) % 4)

            def step_copy(q, s):
                split_lo(ahead(q, s))

            def step_relu(q, s, j, m):
                t = 4 * q + s
                split_lo(ahead(q, s))
                dve.wait_ge(relu_r, j + 1)
                dve.wait_ge(hid_rdy, HR0 + j)
                V.scalar_tensor_tensor(ffv[:, :, :], G[s % 2][:, :, 0:HALF], 0.0, rel[:, s % 2, :, :],
                                       ALU.max, ALU.mult).then_inc(psum_free, 1)
                dve.wait_ge(psum_free, t + 3)
                dve.wait_ge(relu_hi, j + 1)
                V.tensor_tensor(hid_lo[:, ds(m, 1), :, :], ffv[:, :, :].unsqueeze(1),
                                hid_hi[:, ds(m, 1), :, :].bitcast(f32), ALU.subtract).then_inc(hid_rdy, 1)

            def step_resid(q, s, r, m, gate, last=False):
                t = 4 * q + s
                if not last:
                    split_lo(ahead(q, s))
                dve.wait_ge(unit_done, UD0 + t + 1)
                dve.wait_ge(psum_free, t + 2)
                V.tensor_tensor(bt(rtmp[:, :, :]), bt(gs[s % 2]),
                                per_row(adaT[:, ds(gate + m, 1), 1:9].rearrange("p a r -> p (a r)")), ALU.mult).then_inc(res_tmp, 1)
                xp = x[:, ds(m, 1), :, 0:256].rearrange("p a h n -> p (a h) n")
                V.scalar_tensor_tensor(xp, gp[s % 2], adaT[:, ds(gate + m, 1), 0:1].rearrange("p a r -> p (a r)"), xp,
                                       ALU.mult, ALU.add).then_inc(res_tmp, 1)
                dve.wait_ge(res_tmp, 2 * r + 1)
                xs = x[:, ds(m, 1), :, 256:272].rearrange("p a h n -> p (a h) n")
                V.tensor_tensor(xs, xs, rtmp[:, :, :], ALU.add).then_inc(psum_free, 1)

            def ada_turn(g):
                dve.wait_ge(ada_tp, g + 1)
                for m in range(4):
                    ins = V.tensor_tensor(
                        adaT[:, ds(16 * g, 16), :].rearrange("p (j m) r -> p j m r", m=4)[:, :, m, :],
                        TP[:, 128 * m:128 * m + 128].rearrange("p (j r) -> p j r", j=4)[:, :, 0:9],
                        vec[:, ds(16 * g, 16)].rearrange("p (j m) -> p j m", m=4)[:, :, m].unsqueeze(2).broadcast_to([128, 4, 9]),
                        ALU.add)
                ins.then_inc(ada_T, 1)

            def norm_apply(nn, groups, between=None):
                s = norm[nn]
                base = 48 * (nn // 2) + (0 if nn % 2 == 0 else 24)
                dve.wait_ge(ada_T, groups)
                V.scalar_tensor_tensor(amod[:, :, :], adaT[:, base + 8:base + 16, :], 1.0,
                                       vec[:, 96 + 8 * nn:104 + 8 * nn].unsqueeze(2).broadcast_to([128, KC, 9]),
                                       ALU.add, ALU.mult).then_inc(s["mod"], 1)
                dve.wait_ge(s["mod"], 1)
                dve.wait_ge(s["rs"], 2)

                def front(c):
                    if c >= 2:
                        dve.wait_ge(s["hf"], c - 1)
                        dve.wait_ge(s["s1"], c - 1)
                    V.tensor_tensor(uu[:, c % 2, :, :], x[:, c, :, :], rstd[:, :, :], ALU.mult).then_inc(s["u"], 1)

                front(0)
                for c in range(KC):
                    if between and c == 6:
                        between()
                    if c + 1 < KC:
                        front(c + 1)
                    dve.wait_ge(s["hi"], c + 1)
                    V.tensor_tensor(h_lo[:, c, :, :], hf[:, c % 2, :, :], h_hi[:, c, :, :].bitcast(f32),
                                    ALU.subtract).then_inc(s["h"], 1)

            V.memset(cT[:, :, :], 0.0).then_inc(dve_init, 1)
            V.memset(ones[:, :], 1.0).then_inc(dve_init, 1)
            V.memset(eps_t[:, :], EPS).then_inc(dve_init, 1)
            dve.wait_ge(act_c, 2)
            V.tensor_scalar(c_exp[:, :, :], c_exp[:, :, :], 1.0, None, ALU.add).then_inc(dve_c, 1)
            dve.wait_ge(dve_c, 1)
            V.reciprocal(c_exp[:, :, :], c_exp[:, :, :]).then_inc(dve_c, 1)
            dve.wait_ge(dve_c, 2)
            dve.wait_ge(dve_init, 3)
            V.tensor_tensor(cT[:, :, 0:9], c_tr[:, :, :], c_exp[:, :, :], ALU.mult).then_inc(dve_c, 1)
            for c in range(KC):
                dve.wait_ge(pe_x, c + 1)
                V.tensor_copy(x[:, c, :, 0:256], G[c % 2][:, 0, :].rearrange("p (h n) -> p h n", h=2)).then_inc(x_cp, 1)
            dve.wait_ge(pe_vec, 1)
            V.tensor_copy(vec[:, :], TP[:, 0:140]).then_inc(dve_vec, 1)
            split_lo((0, 0))
            split_lo((0, 1))
            dve.wait_ge(dve_vec, 1)
            ada_turn(0)
            norm_apply(0, 1, lambda: split_lo((0, 2)))

            for t in range(12):
                step_copy(t // 4, t % 4)
                if t == 9:
                    ada_turn(1)

            dve.wait_ge(psum_free, 2 + 12)
            V.memset(q_bd[:, :, :], 0.0).then_inc(qz, 1)
            dve.wait_ge(qz, 1)
            with dve.Fori(0, 2) as g:
                base = SD0 + SD_STEPS * g
                n = [0]

                def did(ins):
                    n[0] += 1
                    ins.then_inc(sd, 1)

                def after():
                    dve.wait_ge(sd, base + n[0])

                after()
                for hh in range(2):
                    rows = slice(64 * hh, 64 * hh + 64)
                    qd = q_bd[rows, :, :].rearrange("p r (b h t) -> p r b h t", b=4, h=8)
                    for pr in range(4):
                        ins = V.tensor_scalar(qd[:, pr, :, 2 * pr + hh, :],
                                              ab[rows, pr, ds(g, 1), 256:272].rearrange("p a (b t) -> p (a b) t", t=NT),
                                              1.0, None, ALU.mult)
                ins.then_inc(q_rdy, 1)

                def two_blocks(i):
                    did(V.tensor_reduce(sm[:, 2 * i:2 * i + 2], ST[:, i, :].rearrange("p (b n) -> p b n", b=2), AX.X, ALU.add))
                    did(V.scalar_tensor_tensor(s_sb[:, 512 * i:512 * i + 512].rearrange("p (b n) -> p b n", b=2),
                                               k_row[:, :].unsqueeze(1).broadcast_to([128, 2, 256]), slope_row[:, 0:1],
                                               ST[:, i, :].rearrange("p (b n) -> p b n", b=2), ALU.mult, ALU.add))

                for quarter in range(4):
                    for m in range(8 * quarter + 1, 8 * quarter + 8, 2):
                        b, pg = m // 2 % 4, m % 2
                        dve.wait_ge(page_free, 64 * g + 8 + m + 1)
                        dve.wait_ge(s_pe, 4 * g + quarter) if quarter else None
                        V.tensor_copy(kT[:, :, b, 128 * pg:128 * pg + 128],
                                      KTB[m % 3].rearrange("p (r n) -> p r n", r=4)).then_inc(kt_dve, 1)
                    if quarter == 1:
                        split_lo(ahead(3 + g, 0))
                    if quarter == 2:
                        dve.wait_ge(out_done, 16 * KV_OUT)
                        dve.wait_ge(s_pe, 4 * g + 2)
                        two_blocks(0)
                dve.wait_ge(s_pe, 4 * g + 4)
                two_blocks(1)
                did(V.tensor_tensor(s_sb[:, PAST:], AP[:, 0:16], own_bias[:, :], ALU.add))
                after()
                did(V.tensor_reduce(sm[:, 4:5], sm[:, 0:4], AX.X, ALU.min))
                after()
                did(V.scalar_tensor_tensor(sm[:, 12:16], sm[:, 0:4], sm[:, 4:5], rank4[:, :], ALU.is_le, ALU.mult))
                after()
                did(V.tensor_reduce(sm[:, 5:6], sm[:, 12:16], AX.X, ALU.max))
                after()
                did(V.tensor_scalar(sm[:, 16:20], sm[:, 12:16], sm[:, 5:6], NEG, ALU.is_equal, ALU.mult))
                after()
                did(V.tensor_tensor(sm[:, 20:24], sm[:, 16:20], past_off[:, :], ALU.add))
                after()
                did(V.tensor_reduce(sm[:, 28:29], s_sb[:, PAST:], AX.X, ALU.max))
                for blk in range(4):
                    cols = s_sb[:, 256 * blk:256 * blk + 256]
                    did(V.tensor_tensor_reduce(out=cols, in0=cols, in1=sm[:, 20 + blk:21 + blk].broadcast_to([128, 256]),
                                               scale=1.0, scalar=-3e38, op0=ALU.add, op1=ALU.max,
                                               accum_out=sm[:, 24 + blk:25 + blk]))
                after()
                did(V.tensor_reduce(sm[:, 8:9], sm[:, 24:29], AX.X, ALU.max))
                after()
                did(V.tensor_scalar(sm[:, 9:10], sm[:, 8:9], -SCALE, None, ALU.mult))
                assert n[0] == SD_EXP, n
                dve.wait_ge(s_exp, g + 1)
                did(V.reciprocal(sm[:, 11:12], sm[:, 10:11]))
                after()
                did(V.tensor_scalar(s_sb[:, :], s_sb[:, :], sm[:, 11:12], None, ALU.mult))
                assert n[0] == SD_P, n
                for s in range(1, 4):
                    split_lo(ahead(3 + g, s))
                dve.wait_ge(page_free, 64 * g + 8 + 64)
                did(V.tensor_tensor(o_tmp[:, :], AP, head_mask[:, :], ALU.mult))
                after()
                for dup in range(2):
                    did(V.tensor_reduce(o2[:, dup, :], o_tmp[:, :].rearrange("p (h d) -> p d h", h=8), AX.X, ALU.add))
                assert n[0] == SD_O2, n
                dve.wait_ge(o2_pe, g + 1)
                for hh in range(2):
                    rows = slice(64 * hh, 64 * hh + 64)
                    src = TP[rows, 0:128].rearrange("p (b h t) -> p b h t", b=4, h=8)
                    for pr in range(4):
                        did(V.tensor_scalar(ab[rows, pr, ds(g, 1), 256:272].rearrange("p a (b t) -> p (a b) t", t=NT),
                                            src[:, :, 2 * pr + hh, :], 1.0, None, ALU.mult))
                assert n[0] == SD_STEPS, n

            def maxima(h):
                hp, n = h % 2, MAX_STEPS * h
                if h:
                    dve.wait_ge(a_max, n)
                V.tensor_scalar(dist_h[:, :], dist[:, :], slopes[:, h:h + 1], None, ALU.mult).then_inc(a_max, 1)
                dve.wait_ge(a_max, n + 1)
                if h >= 2:
                    dve.wait_ge(a_tp, 4 * (h - 1))
                    dve.wait_ge(a_nrm, NRM_STEPS * (h - 1))
                dve.wait_ge(a_s, h + 1)
                for i in range(4):
                    w = 128 * (i + 1)
                    V.tensor_tensor_reduce(
                        out=P[:, hp, QOFF[i]:QOFF[i] + w], in0=SCB[i], in1=dist_h[:, 384 - 128 * i:512],
                        scale=1.0, scalar=-3e38, op0=ALU.add, op1=ALU.max, accum_out=pm[:, hp, i:i + 1]).then_inc(a_max, 1)
                dve.wait_ge(a_max, n + 5)
                V.tensor_scalar(pm[:, hp, 4:8], pm[:, hp, 0:4], -SCALE, None, ALU.mult).then_inc(a_max, 1)

            def normalise(h):
                hp = h % 2
                dve.wait_ge(a_exp, 4 * h + 4)
                V.reciprocal(pm[:, hp, 12:16], pm[:, hp, 8:12]).then_inc(a_nrm, 1)
                dve.wait_ge(a_nrm, NRM_STEPS * h + 1)
                for i in range(4):
                    sl = P[:, hp, QOFF[i]:QOFF[i] + 128 * (i + 1)]
                    V.tensor_scalar(sl, sl, pm[:, hp, 12 + i:13 + i], None, ALU.mult).then_inc(a_nrm, 1)

            maxima(0)
            maxima(1)
            normalise(0)
            split_lo(ahead(5, 0))
            for h in range(NH):
                dve.wait_ge(a_tp, 4 * h + 2)
                if h:
                    dve.wait_ge(a_o, h)
                for j in (1, 3):
                    V.tensor_copy(PT[:, PTO[j]:PTO[j] + 512 - 128 * j], PTB[j][:, 0:512 - 128 * j]).then_inc(a_ev2, 1)
                if h + 1 < NH:
                    normalise(h + 1)
                if h + 2 < NH:
                    maxima(h + 2)
                if h % 2 and h < NH - 1:
                    split_lo(ahead(5, (h + 1) // 2))
            for n, c in enumerate(MIX):
                dve.wait_ge(mix_hi, n + 1)
                V.tensor_tensor(h_lo[:, c, :, :], mix_src(c), h_hi[:, c, :, :].bitcast(f32),
                                ALU.subtract).then_inc(mix_rdy, 1)

            for m in range(KC):
                step_resid(T_OUT // 4 + m // 4, m % 4, m, m, 16)
            ada_turn(2)

            def ff(layer, T0, R0):
                J = 32 * layer
                q0 = T0 // 4
                gate = 48 * layer + 40

                def up(b, ada):
                    for s in range(8):
                        step_relu(q0 + 4 * b + s // 4, s % 4, J + 8 * b + s, s)
                    if ada:
                        ada_turn(3 + b)

                def up_short(b):
                    with dve.Fori(0, 2) as i:
                        for s in range(4):
                            step_relu(q0 + 4 * b + i, s, J + 8 * b + 4 * i + s, 4 * i + s)

                def down(b):
                    with dve.Fori(0, 2) as i:
                        for s in range(4):
                            step_resid(q0 + 4 * b + 2 + i, s, R0 + 8 * b + 4 * i + s, 4 * i + s, gate)

                ada = layer == 0
                up(0, ada)
                down(0)
                with dve.Fori(1, 3) as b:
                    up(b, True) if ada else up_short(b)
                    down(b)
                up_short(3)
                for m in range(KC):
                    step_resid(q0 + 14 + m // 4, m % 4, R0 + 24 + m, m, gate, last=T0 + 56 + m + LA >= T_END)

            norm_apply(1, 3)
            ff(0, T_FF0, 8)
            dve.wait_ge(w_pe, 1)
            for half in range(2):
                V.tensor_tensor(ws_T[:, 4 * half:4 * half + 4, :], XA[:, half, :].rearrange("p (g t) -> p g t", g=4),
                                tri[:, :].unsqueeze(1).broadcast_to([128, 4, 128]), ALU.mult).then_inc(w_dve, 1)
            norm_apply(2, 4)
            for t in range(T_C, T_C + 8):
                step_copy(t // 4, t % 4)

            dve.wait_ge(w_pe, 2)
            V.tensor_tensor(ws_blk[:, :, :].rearrange("p g (b t) -> p g b t", t=NT),
                            AP[0:32, 0:32].rearrange("p (g t) -> p g t", t=NT).unsqueeze(2).broadcast_to([32, 8, 8, NT]),
                            blk_mask[:, :].rearrange("p (b t) -> p b t", t=NT).unsqueeze(1).broadcast_to([32, 8, 8, NT]),
                            ALU.mult).then_inc(w_dve, 1)
            dve.wait_ge(gm_in, 32)

            def v_norm(tt):
                m = 128 if tt < 4 else 32
                dve.wait_ge(v_act, 3 * tt + 3)
                dst = vn[:, tt, :] if tt < 4 else vns[:, :]
                V.scalar_tensor_tensor(dst, VB[tt % 2][0:m, :, :].rearrange("p a n -> p (a n)"), vst[0:m, 2, tt:tt + 1],
                                       gv_row[0:m, :], ALU.mult, ALU.mult).then_inc(v_dve, 1)

            def gate(g):
                dve.wait_ge(g_pe, g + 1)
                V.tensor_tensor(gate_s[:, g % 2, :, 0:256].rearrange("p h (a n) -> p h a n", n=128),
                                VB[g % 2][:, 0, :].rearrange("p (h a n) -> p h a n", h=2, a=2),
                                bs_row[:, g, :].unsqueeze(1).unsqueeze(1).broadcast_to([128, 2, 2, 128]), ALU.add).then_inc(g_s, 1)
                V.tensor_tensor(bt(gate_s[:, g % 2, :, 256:272]),
                                VB[g % 2][:, 1, 0:32].rearrange("p (h b t) -> p h b t", h=2, t=NT),
                                bs_row[:, g, 0:NT].unsqueeze(1).unsqueeze(1).broadcast_to([128, 2, 4, NT]), ALU.add).then_inc(g_s, 1)

            for tt in (0, 1):
                v_norm(tt)
            split_lo(ahead((T_C + 8) // 4, 0))
            for tt in (2, 3, 4):
                v_norm(tt)
            gate(0)
            for m in range(8):
                t = T_C + 8 + m
                if m:
                    split_lo(ahead(t // 4, m % 4))
                dve.wait_ge(unit_done, UD0 + t + 1)
                dve.wait_ge(g_s, 2 * m + 2)
                if m:
                    dve.wait_ge(g_lo, m)
                V.tensor_tensor(gated[:, :, :], G[m % 2][:, :, 0:HALF], gate_s[:, m % 2, :, :], ALU.mult).then_inc(psum_free, 1)
                dve.wait_ge(g_hi, m + 1)
                V.tensor_tensor(hid_lo[:, m, :, :], gated[:, :, :], hid_hi[:, m, :, :].bitcast(f32),
                                ALU.subtract).then_inc(g_lo, 1)
                if m < 7:
                    gate(m + 1)

            for m in range(KC):
                step_resid(T_OUTC // 4 + m // 4, m % 4, 40 + m, m, 48 + 16)
            norm_apply(3, 6)
            V.memset(fin_ss[:, :, :], 0.0).then_inc(fin["zero"], 1)
            ff(1, T_FF1, 48)

            dve.wait_ge(fin["sq"], KC)
            V.tensor_reduce(fin_r[:, 0, :], fin_ss[:, :, :].rearrange("p c t -> p t c"), AX.X, ALU.add).then_inc(fin["rs"], 1)
            dve.wait_ge(fin["g"], 16)
            dve.wait_ge(fin["rs"], 3)
            for tt in range(5):
                m = 128 if tt < 4 else 32
                V.scalar_tensor_tensor(y_all[0:m, tt, :], y_all[0:m, tt, :], fin_r[0:m, 2, tt:tt + 1], gf_row[0:m, :],
                                       ALU.mult, ALU.mult).then_inc(fin["y"], 1)

        @block.tensor
        def _(pe):
            mm, tr = nc.tensor.matmul, nc.tensor.transpose

            def products(t, s, slot, k, rhs_hi, rhs_lo, first, last):
                for w, r in ((w_hi, rhs_hi), (w_hi, rhs_lo), (w_lo, rhs_hi)):
                    for half in range(2):
                        ins = mm(G[slot][:, half, 0:HALF], w[:, s, k, :], r[:, k, half, :],
                                 start=(first and w is w_hi and r is rhs_hi), stop=(last and w is w_lo))
                if last:
                    ins.then_inc(unit_done, 1)

            def unit(q, s, rhs_hi, rhs_lo, wait_k=None, slot=None, korder=range(KC)):
                t = 4 * q + s
                pe.wait_ge(lo_done, t + 1)
                pe.wait_ge(psum_free, t + 1 if slot is None else t + 2)
                for n, k in enumerate(korder):
                    if wait_k:
                        wait_k(n)
                    products(t, s, s % 2 if slot is None else slot, k, rhs_hi, rhs_lo, n == 0, n == KC - 1)

            def pair(q, rhs_hi, rhs_lo, wait_k, korder=range(KC)):
                t = 4 * q
                pe.wait_ge(lo_done, t + 2)
                pe.wait_ge(psum_free, t + 2)
                for n, k in enumerate(korder):
                    wait_k(n)
                    for s in range(2):
                        products(t + s, s, s, k, rhs_hi, rhs_lo, n == 0, n == KC - 1)

            def ada_chunk(g, k, first=False):
                pe.wait_ge(ada_in[k % 2], 64 * (g - 1) + 16 * (k // 2) + 16)
                if k == 0:
                    pe.wait_ge(ada_copied, g)
                for j in range(4):
                    ins = mm(AP[32 * j:32 * j + 32, :], cT[:, k, :], ada_w[:, k % 2, 512 * j:512 * j + 512],
                             start=(k == 0), stop=(k == KC - 1))
                ins.then_inc(ada_used, 1)

            def ada_turn(g):
                pe.wait_ge(ada_copied, g + 1)
                pe.wait_ge(ada_T, g)
                for m in range(4):
                    ins = tr(TP[:, 128 * m:128 * m + 128], ada_sb[:, 128 * m:128 * m + 128], ident[:, :])
                ins.then_inc(ada_tp, 1)

            def norm_stats(s):
                pe.wait_ge(s["acc"], 6)
                pe.wait_ge(s["sq"], 7)
                for half in range(2):
                    mm(ST[:, half, 0:HALF], ones[:, :], ssq[:, half, :], start=True, stop=False)
                pe.wait_ge(s["sq"], 8)
                for half in range(2):
                    ins = mm(ST[:, half, 0:HALF], ones[:, :], sq[:, 1, half, :], start=False, stop=True)
                ins.then_inc(s["st"], 1)

            pe.sem_inc(psum_free, 2)
            pe.sem_inc(page_free, 8)
            pe.sem_inc(unit_done, UD0)
            pe.sem_inc(hid_rdy, HR0)
            pe.sem_inc(sd, SD0)
            pe.wait_ge(c_in, 48)
            for k in range(KC):
                ins = tr(AP[:, 9 * k:9 * k + 9], c_rows[:, 128 * k:128 * k + 128], ident[0:9, 0:9])
            ins.then_inc(pe_c, 1)
            pe.wait_ge(x_in, 80)
            for c in range(KC):
                if c >= 2:
                    pe.wait_ge(x_cp, c - 1)
                    pe.wait_ge(x_cs, c - 1)
                for tt in range(4):
                    tr(G[c % 2][:, 0, 128 * tt:128 * tt + 128], x_tok[:, tt, 128 * c:128 * c + 128], ident[:, :])
                tr(G[c % 2][:, 1, 0:32], xs_tok[:, 128 * c:128 * c + 128], ident[0:32, 0:32]).then_inc(pe_x, 1)
            pe.wait_ge(vec_in, 48)
            tr(TP[:, 0:128], vec_rows[:, :], ident[:, :])
            tr(TP[:, 128:140], vec_rows2[:, :], ident[0:12, 0:12]).then_inc(pe_vec, 1)
            pe.wait_ge(dve_init, 3)
            pe.wait_ge(dve_c, 3)
            for k in range(KC):
                pe.wait_ge(ada0_in[k], 16)
                for j in range(4):
                    ins = mm(AP[32 * j:32 * j + 32, :], cT[:, k, :], ADA0[k][:, 512 * j:512 * j + 512],
                             start=(k == 0), stop=(k == KC - 1))
                ins.then_inc(ada_used, 1)
                if k == 4:
                    norm_stats(norm[0])
            pe.wait_ge(dve_vec, 1)
            ada_turn(0)

            def from_norm(n):
                return lambda k: pe.wait_ge(norm[n]["h"], k + 1)

            def with_ada(g, T, rhs_hi, rhs_lo, wait_k, korder=range(KC), at=((0, 1), (2,), (3,), (4,), (5,), (6,), (7,))):
                for c in at[0]:
                    ada_chunk(g, c)
                pair(T // 4, rhs_hi, rhs_lo, wait_k, korder)
                for s in range(2, 8):
                    for c in at[s - 1]:
                        ada_chunk(g, c)
                    unit(T // 4 + s // 4, s % 4, rhs_hi, rhs_lo, None, None, korder)
                ada_turn(g)

            pair(0, h_hi, h_lo, from_norm(0))
            for t in range(2, 12):
                if t < 10:
                    ada_chunk(1, t - 2)
                unit(t // 4, t % 4, h_hi, h_lo)
                if t == 9:
                    ada_turn(1)

            pe.wait_ge(psum_free, 2 + 12)
            pe.wait_ge(ada_T, 2)
            for i in range(4):
                c0, g = (8, i) if i < 2 else (4, i - 2)
                for ch in range(4):
                    ins = tr(TMA[i][0:16, 128 * ch:128 * ch + 128], ab[:, c0 + ch, g, 256:272], ident[:, :])
                ins.then_inc(tma_pe, 1)

            pe.wait_ge(tma_ev, 4)
            with pe.Fori(0, 2) as g:
                def quarter_scores(quarter):
                    pe.wait_ge(kt_act, 16 * g + 4 * quarter + 4)
                    pe.wait_ge(kt_dve, 16 * g + 4 * quarter + 4)
                    cols = slice(256 * (quarter % 2), 256 * (quarter % 2) + 256)
                    for pr in range(4):
                        for b in range(4):
                            ins = mm(ST[32 * b:32 * b + 32, quarter // 2, cols], q_bd[:, pr, 32 * b:32 * b + 32],
                                     kT[:, pr, b, :], start=(pr == 0), stop=(pr == 3))
                    ins.then_inc(s_pe, 1)

                for n in range(32):
                    slot = n % 8
                    pe.wait_ge(pg_in[slot], 128 * g + 16 * (n // 8) + 16)
                    if n >= 3:
                        pe.wait_ge(kt_act if n % 2 else kt_dve, 16 * g + (n - 3) // 2 + 1)
                    for pr in range(4):
                        ins = tr(KTB[n % 3][:, 128 * pr:128 * pr + 128], kv_ring[:, slot, 128 * pr:128 * pr + 128],
                                 ident[:, :])
                    ins.then_inc(page_free, 1)
                    if n == 1:
                        pe.wait_ge(q_rdy, g + 1)
                        pe.wait_ge(sd, SD0 + SD_STEPS * g)
                        for pr in range(4):
                            mm(AP[:, 0:16], q_bd[:, pr, :], ab[:, 4 + pr, ds(g, 1), 256:272].rearrange("p a n -> p (a n)"),
                               start=(pr == 0), stop=(pr == 3))
                    if n > 8 and n % 8 == 2:
                        quarter_scores(n // 8 - 1)
                quarter_scores(3)
                unit(3 + g, 0, h_hi, h_lo, slot=0)
                pe.wait_ge(sd, SD0 + SD_STEPS * g + SD_P)
                for n in range(9):
                    if n >= 3:
                        pe.wait_ge(p_act, 9 * g + n - 2)
                    if n < 8:
                        tr(PTT[n % 3][:, 0:128], s_sb[:, 128 * n:128 * n + 128], ident[:, :]).then_inc(p_pe, 1)
                    else:
                        tr(PTT[n % 3][0:16, 0:128], s_sb[:, PAST:], ident[:, :]).then_inc(p_pe, 1)
                pe.wait_ge(p_act, 9 * g + 9)
                mm(AP, pT_own[:, :], v_own[:, ds(g, 1), :].rearrange("p a n -> p (a n)"), start=True, stop=False,
                   skip_group_check=True)

                def v_page(n):
                    slot, j, b = n % 8, n // 4, n % 4
                    pe.wait_ge(pg_in[slot], 128 * g + 64 + 16 * (n // 8) + 16)
                    mm(AP[32 * b:32 * b + 32, :], pT[:, j, 32 * b:32 * b + 32], kv_ring[:, slot, :],
                       start=False, stop=(j == 7), skip_group_check=True).then_inc(page_free, 1)

                for n in range(8):
                    v_page(n)
                unit(3 + g, 1, h_hi, h_lo, lambda k: v_page(8 + k), slot=0)
                unit(3 + g, 2, h_hi, h_lo, lambda k: v_page(16 + k), slot=0)
                for n in range(24, 32):
                    v_page(n)
                unit(3 + g, 3, h_hi, h_lo, slot=0)
                pe.wait_ge(sd, SD0 + SD_STEPS * g + SD_O2)
                tr(TP[:, 0:128], o2[:, :, :].rearrange("p a d -> p (a d)"), ident[:, :]).then_inc(o2_pe, 1)

            for i in range(8):
                if i == 4:
                    pe.wait_ge(sd, SD0 + 2 * SD_STEPS)
                    pe.wait_ge(st_in, 16)
                    for ch in range(4):
                        ins = tr(AP[:, 16 * ch:16 * ch + 16], st_rows[:, 128 * ch:128 * ch + 128], ident[0:16, 0:16])
                    ins.then_inc(cv_pe, 1)
                if i in TMB_USED:
                    pe.wait_ge(tmb_ev, TMB_USED[i])
                for ch in range(4):
                    ins = tr(TMB[i][:, 128 * ch:128 * ch + 128], tok(ab, (4 if i < 4 else 8) + ch, i % 4), ident[:, :])
                ins.then_inc(tmb_pe, 1)
            pe.wait_ge(cv_ev, 1)

            def scores(h):
                rows, pr = slice(64 * (h % 2), 64 * (h % 2) + 64), h // 2
                if h:
                    pe.wait_ge(a_max, MAX_STEPS * (h - 1) + 5)
                for i in (0, 2, 3, 1):
                    q = tok(ab, pr, i)[rows, :]
                    if i == 1 and h >= 2:
                        pe.wait_ge(a_ev, 2 * (h - 2) + 1)
                    if i < 2:
                        ins = mm(SCB[i], q, ab[rows, 4 + pr, 0, 0:128 * (i + 1)], start=True, stop=True)
                    elif i == 2:
                        mm(SCB[i][:, 0:256], q, ab[rows, 4 + pr, 0, 0:256], start=True, stop=True)
                        mm(SCB[i][:, 256:384], q, ab[rows, 4 + pr, 1, 0:128], start=True, stop=True)
                    else:
                        mm(SCB[i], q, ab[rows, 4 + pr, :, 0:256], start=True, stop=True)
                ins.then_inc(a_s, 1)

            def half_unit(h):
                s, k0 = h // 2, KC // 2 * (h % 2)
                if k0 == 0:
                    pe.wait_ge(lo_done, 20 + s + 1)
                    pe.wait_ge(psum_free, 20 + s + 2)
                for k in range(k0, k0 + KC // 2):
                    products(20 + s, s, 0, k, h_hi, h_lo, k == 0, k == KC - 1)

            scores(0)
            half_unit(0)
            scores(1)
            half_unit(1)
            pe.wait_ge(tmb_ev, 8)
            for h in range(NH):
                pe.wait_ge(a_nrm, NRM_STEPS * (h + 1))
                if h + 1 < NH:
                    pe.wait_ge(a_max, MAX_STEPS * (h + 1) + 5)
                for j in (1, 3, 2, 0):
                    for i in range(j, 4):
                        ins = tr(PTB[j][:, 128 * (i - j):128 * (i - j) + 128],
                                 P[:, h % 2, QOFF[i] + 128 * j:QOFF[i] + 128 * j + 128], ident[:, :])
                    ins.then_inc(a_tp, 1)
                if h + 2 < NH:
                    scores(h + 2)
                if h in HALF_AT:
                    half_unit(HALF_AT[h])
                pe.wait_ge(a_ev, 2 * h + 2)
                pe.wait_ge(a_ev2, 2 * h + 2)
                if h % 2 == 0 and h:
                    pe.wait_ge(a_out, h // 2)
                rows = slice(64 * (h % 2), 64 * (h % 2) + 64)
                for j in range(4):
                    ins = mm(OUTB[rows, 128 * j:512], v_tok[:, j, 64 * h:64 * h + 64], PT[:, PTO[j]:PTO[j] + 512 - 128 * j],
                             start=(j == 0), stop=(j == 3), skip_group_check=True)
                ins.then_inc(a_o, 1)
            pe.wait_ge(cv, 4 * CV_STEPS)
            for ch in range(4):
                ins = tr(TP[0:18, 128 * ch:128 * ch + 128], cv_state[:, ch, :], ident[:, :])
            ins.then_inc(cv_pe, 1)

            with_ada(2, T_OUT, h_hi, h_lo, lambda n: pe.wait_ge(mix_rdy, n + 1), MIX,
                     ((), (0, 1), (2,), (3, 4), (5,), (6,), (7,)))

            def token_turn(c, T):
                pe.wait_ge(psum_free, 2 + T + c + 1)
                if c >= 2:
                    pe.wait_ge(fin["sq"], c - 1)
                for tt in range(4):
                    tr(VB[c % 2][:, 0, 128 * tt:128 * tt + 128], tok(x, c, tt), ident[:, :])
                pe.wait_ge(fin["smp"], c + 1)
                ins = tr(VB[c % 2][0:32, 1, 0:128], x_smp[:, c % 2, :], ident[:, :])
                ins.then_inc(fin["tp"], 1)

            def ff(layer, T0, nn):
                J = 32 * layer
                q0 = T0 // 4

                def down(b):
                    def hid(k):
                        pe.wait_ge(hid_rdy, HR0 + J + 8 * b + k + 1)
                    with pe.Fori(0, 2) as i:
                        for s in range(4):
                            unit(q0 + 4 * b + 2 + i, s, hid_hi, hid_lo, hid if s == 0 else None)

                def up_ada(b):
                    for s in range(8):
                        ada_chunk(3 + b, s)
                        unit(q0 + 4 * b + s // 4, s % 4, h_hi, h_lo)
                    ada_turn(3 + b)

                def up(b):
                    with pe.Fori(0, 2) as i:
                        for s in range(4):
                            unit(q0 + 4 * b + i, s, h_hi, h_lo)

                if layer == 0:
                    with_ada(3, T0, h_hi, h_lo, from_norm(nn), at=((0, 1), (), (2,), (3,), (4, 5), (6,), (7,)))
                else:
                    pair(q0, h_hi, h_lo, from_norm(nn))
                    for s in range(2, 8):
                        unit(q0 + s // 4, s % 4, h_hi, h_lo)
                down(0)
                with pe.Fori(1, 3) as b:
                    up_ada(b) if layer == 0 else up(b)
                    down(b)
                up(3)
                if layer == 0:
                    down(3)
                    return
                for s in range(8):
                    unit(q0 + 14 + s // 4, s % 4, hid_hi, hid_lo,
                         (lambda k: pe.wait_ge(hid_rdy, HR0 + J + 24 + k + 1)) if s == 0 else None)
                    if s:
                        token_turn(s - 1, T0 + 56)
                token_turn(KC - 1, T0 + 56)

            norm_stats(norm[1])
            ff(0, T_FF0, 1)
            pe.wait_ge(ws_in, 16)
            pe.wait_ge(ada_T, 6)
            for g in range(8):
                ins = tr(XA[:, g // 4, 128 * (g % 4):128 * (g % 4) + 128], ws_raw[:, g, :], ident[:, :])
            ins.then_inc(w_pe, 1)
            norm_stats(norm[2])
            pair(T_C // 4, h_hi, h_lo, from_norm(2))
            pe.wait_ge(w_dve, 2)
            mm(AP[0:32, 0:32], rep4[:, :], ws_T[0:4, :, 0:4], start=True, stop=True).then_inc(w_pe, 1)
            for s in range(2, 8):
                unit(T_C // 4 + s // 4, s % 4, h_hi, h_lo)

            pe.wait_ge(psum_free, 2 + T_C + 8)
            pe.wait_ge(w_dve, 3)

            def v_turn(tt):
                if tt >= 2:
                    pe.wait_ge(v_dve, tt - 1)
                if tt == 4:
                    pe.wait_ge(v_rows, 1)
                for ch in range(KC):
                    m = 128 if tt < 4 else 32
                    src = tok(v_T, ch, tt) if tt < 4 else v_smp[:, ch, :]
                    ins = tr(VB[tt % 2][0:m, ch // 4, 128 * (ch % 4):128 * (ch % 4) + 128], src, ident[:, :])
                ins.then_inc(v_pe, 1)

            def spatial(g):
                pe.wait_ge(v_dve, 5)
                if g >= 2:
                    pe.wait_ge(g_s, 2 * (g - 1))
                for tt in range(4):
                    mm(VB[g % 2][:, 0, 128 * tt:128 * tt + 128], vn[:, tt, 128 * g:128 * g + 128], ws_T[:, g, :],
                       start=True, stop=True)
                mm(VB[g % 2][:, 1, 0:32], vns[:, 128 * g:128 * g + 128], ws_blk[:, g, :], start=True, stop=True).then_inc(g_pe, 1)

            v_turn(0)
            v_turn(1)
            q0 = (T_C + 8) // 4
            unit(q0, 0, h_hi, h_lo, lambda k: v_turn(2) if k == 4 else None)
            unit(q0, 1, h_hi, h_lo, lambda k: v_turn(3 + k // 4) if k % 4 == 0 else None)
            spatial(0)
            for m in range(2, 8):
                spatial(m - 1)
                if m == 7:
                    spatial(7)
                unit(q0 + m // 4, m % 4, h_hi, h_lo)

            def gated_rdy(k):
                pe.wait_ge(g_lo, k + 1)
            pair(T_OUTC // 4, hid_hi, hid_lo, gated_rdy)
            for s in range(2, 8):
                unit(T_OUTC // 4 + s // 4, s % 4, hid_hi, hid_lo)
            norm_stats(norm[3])
            ff(1, T_FF1, 3)


def kernel(x_prompt, x_sample, cache_k, cache_v, state_conv, page_table, c_prompt, c_sample, norm_g, w_ada, b_ada,
           w_in_ab, conv_w, w_out_ab, w_in_c, g_v, w_s, b_s, w_out_c, w_ff1, w_ff2, g_final):
    import numpy as _np
    import concourse.bacc as _bacc
    from concourse import mybir as _mybir
    from concourse.bass_utils import run_bass_kernel_spmd as _run

    f = _np.float32
    p = _np.arange(128)
    c = _np.arange(512)
    slope = _np.exp2(-8.0 * _np.arange(1, NH + 1) / NH)
    row_b, row_h, row_t = p // 32, p // 4 % 8, p % 4
    own = _np.arange(16)
    own_d = row_t[:, None] - own[None, :] % 4
    own_ok = (own[None, :] // 4 == row_b[:, None]) & (own_d >= 0)
    r32 = _np.arange(32)
    consts = {
        "k_ident": _np.eye(128),
        "k_dist": _np.where(c[None, :] - 384 <= p[:, None], c[None, :] - 384 - p[:, None], NEG),
        "k_head_mask": c[None, :] // HD == row_h[:, None],
        "k_own_bias": _np.where(own_ok, -own_d * slope[row_h][:, None] / SCALE, NEG),
        "k_row": _np.broadcast_to(_np.arange(256) - 255, (128, 256)),
        "k_slope_row": (slope[row_h] / SCALE)[:, None],
        "k_past_off": -(PAST + row_t[:, None] - 256 * _np.arange(4)[None, :] - 255) * slope[row_h][:, None] / SCALE,
        "k_slopes": _np.broadcast_to(slope / SCALE, (128, NH)),
        "k_rank4": _np.broadcast_to(_np.arange(1, 5), (128, 4)),
        "k_rep4": r32[None, :] % 4 == _np.arange(4)[:, None],
        "k_blk_mask": r32[:, None] // 4 == r32[None, :] // 4,
        "k_tri": p[:, None] <= p[None, :],
    }
    arrays = {n: _np.ascontiguousarray(v.astype(f)) for n, v in consts.items()}
    pt = _np.asarray(page_table).reshape(2, 4, 4, 2)
    k_order = pt.transpose(0, 2, 1, 3).reshape(2, 32)
    v_order = pt.reshape(2, 4, 8).transpose(0, 2, 1).reshape(2, 32)
    arrays["page_order"] = _np.ascontiguousarray(_np.concatenate([k_order, v_order], 1).reshape(1, 128))
    given = dict(x_prompt=x_prompt, x_sample=x_sample, cache_k=cache_k, cache_v=cache_v, state_conv=state_conv,
                 c_prompt=c_prompt, c_sample=c_sample, norm_g=norm_g, w_ada=w_ada, b_ada=b_ada, w_in_ab=w_in_ab,
                 conv_w=conv_w, w_out_ab=w_out_ab, w_in_c=w_in_c, g_v=g_v, w_s=w_s, b_s=b_s, w_out_c=w_out_c,
                 w_ff1=w_ff1, w_ff2=w_ff2, g_final=g_final)
    for n, v in given.items():
        arrays[n] = _np.ascontiguousarray(v)

    nc = _bacc.Bacc("TRN2", target_bir_lowering=False, num_devices=1)
    a = {n: nc.dram_tensor("in_" + n, v.shape, _mybir.dt.from_np(v.dtype), kind="ExternalInput").ap()
         for n, v in arrays.items()}
    shapes = [("y_prompt", (1, SEQ, D)), ("y_sample", (NB, NT, D)),
              ("k_prompt", (1, SEQ // PAGE, PAGE, NH, HD)), ("v_prompt", (1, SEQ // PAGE, PAGE, NH, HD)),
              ("conv_prompt", (1, 1, 2, D // 2)),
              ("k_sample", (1, NB, NT, NH, HD)), ("v_sample", (1, NB, NT, NH, HD)),
              ("conv_sample", (1, NB, 2, D // 2)), ("cv_sample", (1, NB, NT, D))]
    out = {n: nc.dram_tensor("out_" + n, s, _mybir.dt.float32, kind="ExternalOutput").ap() for n, s in shapes}
    trunk_kernel(nc, a, out)
    r = _run(nc, [{"in_" + n: v for n, v in arrays.items()}], core_ids=[0])
    return tuple(r.results[0]["out_" + n] for n, _ in shapes)
```
